# Optimizing a Trainium2 kernel written in Bass

```python
import math
import jax
import jax.numpy as jnp
from jax import lax
import numpy as np

D_MODEL = 2048
BATCH = 1
SEQ = 256
DEPTH = 1

CHUNK = 64
N_META = 16
CONV_WIDTH = D_MODEL // 2
CONV_GROUPS = 8
CONV_KERNEL = 31
HEAD_DIM = 128
N_DELTA_HEADS = (D_MODEL // 2) // HEAD_DIM
DELTA_WIDTH = N_DELTA_HEADS * HEAD_DIM
SHORT_CONV = 4
MIX_WIDTH = CONV_WIDTH + DELTA_WIDTH
N_GROUPS = 4
EXPERTS_PER_GROUP = 8
N_EXPERTS = N_GROUPS * EXPERTS_PER_GROUP
TOP_K = 2
D_EXPERT = 512
EPS = 1e-6
IN_COLS = 2 * CONV_WIDTH + 4 * DELTA_WIDTH + 2 * N_DELTA_HEADS

kernel_name = 'hybrid_conformer_deltanet_hmoe'

def rmsnorm(x, g):
    xf = x.astype(jnp.float32)
    y = xf * lax.rsqrt(jnp.mean(xf * xf, axis=-1, keepdims=True) + EPS)
    return (y * g.astype(jnp.float32)).astype(x.dtype)

def causal_depthwise_conv(x, w):
    k = w.shape[0]
    xp = jnp.pad(x, ((0, 0), (k - 1, 0), (0, 0)))
    return lax.conv_general_dilated(
        xp, w[:, None, :].astype(x.dtype), window_strides=(1,), padding='VALID',
        dimension_numbers=('NWC', 'WIO', 'NWC'), feature_group_count=x.shape[-1])

def split_in_proj(p):
    c, dl, h = CONV_WIDTH, DELTA_WIDTH, N_DELTA_HEADS
    idx = [c, 2 * c, 2 * c + 3 * dl, 2 * c + 4 * dl, 2 * c + 4 * dl + h]
    return jnp.split(p, idx, axis=-1)

def conformer_conv(glu_a, glu_b, w_dw, b_dw, ln_g, ln_b):
    y = glu_a * jax.nn.sigmoid(glu_b)
    y = causal_depthwise_conv(y, w_dw) + b_dw.astype(y.dtype)
    b_, l_, _ = y.shape
    yg = y.reshape(b_, l_, CONV_GROUPS, CONV_WIDTH // CONV_GROUPS).astype(jnp.float32)
    mu = jnp.mean(yg, axis=-1, keepdims=True)
    var = jnp.mean(jnp.square(yg - mu), axis=-1, keepdims=True)
    yg = (yg - mu) * lax.rsqrt(var + EPS)
    y = yg.reshape(b_, l_, CONV_WIDTH) * ln_g.astype(jnp.float32) + ln_b.astype(jnp.float32)
    return jax.nn.silu(y).astype(glu_a.dtype)

def chunk_gated_delta_rule(q, k, v, beta, g):
    b_, l_, h_, d_ = q.shape
    pad = (-l_) % CHUNK

    def prep(t):
        t = jnp.pad(t, ((0, 0), (pad, 0)) + ((0, 0),) * (t.ndim - 2))
        t = t.reshape((b_, -1, CHUNK) + t.shape[2:])
        return jnp.moveaxis(t, 3, 2)

    q, k, v, beta, g = prep(q), prep(k), prep(v), prep(beta), prep(g)
    gc = jnp.cumsum(g, axis=-1)
    incl = jnp.tril(jnp.ones((CHUNK, CHUNK), dtype=bool))
    strict = jnp.tril(jnp.ones((CHUNK, CHUNK), dtype=bool), -1)
    decay = jnp.exp(jnp.where(incl, gc[..., :, None] - gc[..., None, :], -jnp.inf))
    kb = k * beta[..., None]
    vb = v * beta[..., None]
    m = jnp.einsum('bnhid,bnhjd->bnhij', kb, k) * decay
    a_mat = jnp.where(strict, m, 0.0) + jnp.eye(CHUNK, dtype=jnp.float32)
    rhs = jnp.concatenate([vb, kb * jnp.exp(gc)[..., None]], axis=-1)
    sol = lax.linalg.triangular_solve(a_mat, rhs, left_side=True, lower=True, unit_diagonal=True)
    u, w = sol[..., :d_], sol[..., d_:]
    intra = jnp.einsum('bnhid,bnhjd->bnhij', q, k) * decay
    q_dec = q * jnp.exp(gc)[..., None]
    k_dec = k * jnp.exp(gc[..., -1:] - gc)[..., None]
    g_last = jnp.exp(gc[..., -1])
    xs = tuple(jnp.moveaxis(t, 1, 0) for t in (u, w, q_dec, k_dec, intra, g_last))

    def step(s, inp):
        u_c, w_c, qd_c, kd_c, intra_c, gl_c = inp
        v_new = u_c - jnp.einsum('bhcd,bhde->bhce', w_c, s)
        o_c = jnp.einsum('bhcd,bhde->bhce', qd_c, s) + jnp.einsum('bhij,bhje->bhie', intra_c, v_new)
        s = s * gl_c[..., None, None] + jnp.einsum('bhcd,bhce->bhde', kd_c, v_new)
        return s, o_c

    s0 = jnp.zeros((b_, h_, d_, d_), jnp.float32)
    _, o = lax.scan(step, s0, xs)
    o = jnp.transpose(o, (1, 0, 3, 2, 4)).reshape(b_, -1, h_, d_)
    return o[:, pad:]

def gated_deltanet(qkv, z, beta_logit, decay_logit, sc_w, a_log, dt_bias, norm_g):
    b_, l_, _ = qkv.shape
    qkv = jax.nn.silu(causal_depthwise_conv(qkv, sc_w))
    q, k, v = (t.reshape(b_, l_, N_DELTA_HEADS, HEAD_DIM).astype(jnp.float32)
               for t in jnp.split(qkv, 3, axis=-1))
    q = q * lax.rsqrt(jnp.sum(q * q, axis=-1, keepdims=True) + EPS) * (HEAD_DIM ** -0.5)
    k = k * lax.rsqrt(jnp.sum(k * k, axis=-1, keepdims=True) + EPS)
    beta = jax.nn.sigmoid(beta_logit.astype(jnp.float32))
    g = -jnp.exp(a_log.astype(jnp.float32)) * jax.nn.softplus(
        decay_logit.astype(jnp.float32) + dt_bias.astype(jnp.float32))
    o = chunk_gated_delta_rule(q, k, v, beta, g)
    o = o * lax.rsqrt(jnp.mean(o * o, axis=-1, keepdims=True) + EPS) * norm_g.astype(jnp.float32)
    o = o * jax.nn.silu(z.reshape(b_, l_, N_DELTA_HEADS, HEAD_DIM).astype(jnp.float32))
    return o.reshape(b_, l_, DELTA_WIDTH).astype(z.dtype)

def hier_moe(u, w_group, b_group, w_router, b_router, w_gate, w_up, w_down):
    b_, l_, d_ = u.shape
    t = u.reshape(-1, d_)
    glog = (t @ w_group).astype(jnp.float32) + b_group.astype(jnp.float32)
    gprob = jax.nn.softmax(glog, axis=-1)
    gsel = jnp.argmax(glog, axis=-1)
    p_group = jnp.take_along_axis(gprob, gsel[:, None], axis=-1)
    elog = ((t @ w_router).astype(jnp.float32) + b_router.astype(jnp.float32)).reshape(
        -1, N_GROUPS, EXPERTS_PER_GROUP)
    elog_sel = jnp.take_along_axis(elog, gsel[:, None, None], axis=1)[:, 0]
    top_v, top_i = lax.top_k(elog_sel, TOP_K)
    w_k = jax.nn.softmax(top_v, axis=-1) * p_group
    within = jnp.sum(jax.nn.one_hot(top_i, EXPERTS_PER_GROUP, dtype=jnp.float32) * w_k[..., None], axis=1)
    comb = jax.nn.one_hot(gsel, N_GROUPS, dtype=jnp.float32)[:, :, None] * within[:, None, :]
    comb = comb.reshape(-1, N_EXPERTS).astype(t.dtype)
    out = jnp.zeros_like(t)
    for gi in range(N_GROUPS):
        sl = slice(gi * EXPERTS_PER_GROUP, (gi + 1) * EXPERTS_PER_GROUP)
        hg = jnp.einsum('nd,edf->nef', t, w_gate[sl])
        hu = jnp.einsum('nd,edf->nef', t, w_up[sl])
        hid = jax.nn.silu(hg) * hu * comb[:, sl, None]
        out = out + jnp.einsum('nef,efd->nd', hid, w_down[sl])
    return out.reshape(b_, l_, d_)

def setup_inputs(seed: int = 0) -> dict:
    key = jax.random.key(seed)
    ks = jax.random.split(key, 24)
    f32 = jnp.float32

    def nrm(k, shape, scale):
        return jax.random.normal(k, shape, f32) * scale

    dt = jnp.exp(jax.random.uniform(ks[9], (DEPTH, N_DELTA_HEADS), f32, math.log(1e-3), math.log(1e-1)))
    return {
        'x': nrm(ks[0], (BATCH, SEQ, D_MODEL), 1.0),
        'meta': nrm(ks[1], (N_META, D_MODEL), 1.0),
        'attn_norm': 1.0 + nrm(ks[2], (DEPTH, D_MODEL), 0.02),
        'w_in': nrm(ks[3], (DEPTH, D_MODEL, IN_COLS), D_MODEL ** -0.5),
        'conv_dw_w': nrm(ks[4], (DEPTH, CONV_KERNEL, CONV_WIDTH), CONV_KERNEL ** -0.5),
        'conv_dw_b': nrm(ks[5], (DEPTH, CONV_WIDTH), 0.02),
        'conv_ln_g': 1.0 + nrm(ks[6], (DEPTH, CONV_WIDTH), 0.02),
        'conv_ln_b': nrm(ks[7], (DEPTH, CONV_WIDTH), 0.02),
        'short_conv_w': nrm(ks[8], (DEPTH, SHORT_CONV, 3 * DELTA_WIDTH), SHORT_CONV ** -0.5),
        'a_log': jnp.log(jax.random.uniform(ks[10], (DEPTH, N_DELTA_HEADS), f32, 1.0, 16.0)),
        'dt_bias': dt + jnp.log(-jnp.expm1(-dt)),
        'delta_norm_g': 1.0 + nrm(ks[11], (DEPTH, HEAD_DIM), 0.02),
        'w_out': nrm(ks[12], (DEPTH, MIX_WIDTH, D_MODEL), MIX_WIDTH ** -0.5),
        'ffn_norm': 1.0 + nrm(ks[13], (DEPTH, D_MODEL), 0.02),
        'w_group': nrm(ks[14], (DEPTH, D_MODEL, N_GROUPS), D_MODEL ** -0.5),
        'b_group': nrm(ks[15], (DEPTH, N_GROUPS), 0.01),
        'w_router': nrm(ks[16], (DEPTH, D_MODEL, N_EXPERTS), D_MODEL ** -0.5),
        'b_router': nrm(ks[17], (DEPTH, N_EXPERTS), 0.01),
        'w_gate': nrm(ks[18], (DEPTH, N_EXPERTS, D_MODEL, D_EXPERT), D_MODEL ** -0.5),
        'w_up': nrm(ks[19], (DEPTH, N_EXPERTS, D_MODEL, D_EXPERT), D_MODEL ** -0.5),
        'w_down': nrm(ks[20], (DEPTH, N_EXPERTS, D_EXPERT, D_MODEL), D_EXPERT ** -0.5),
        'final_norm': 1.0 + nrm(ks[21], (D_MODEL,), 0.02),
    }

def reference(x, meta, attn_norm, w_in, conv_dw_w, conv_dw_b, conv_ln_g, conv_ln_b,
              short_conv_w, a_log, dt_bias, delta_norm_g, w_out, ffn_norm, w_group,
              b_group, w_router, b_router, w_gate, w_up, w_down, final_norm):
    b_ = x.shape[0]
    meta_b = jnp.broadcast_to(meta[None].astype(x.dtype), (b_, N_META, D_MODEL))
    h = jnp.concatenate([meta_b, x], axis=1)
    for l in range(DEPTH):
        u = rmsnorm(h, attn_norm[l])
        glu_a, glu_b, qkv, z, beta_logit, decay_logit = split_in_proj(u @ w_in[l])
        y_conv = conformer_conv(glu_a, glu_b, conv_dw_w[l], conv_dw_b[l], conv_ln_g[l], conv_ln_b[l])
        y_delta = gated_deltanet(qkv, z, beta_logit, decay_logit, short_conv_w[l],
                                 a_log[l], dt_bias[l], delta_norm_g[l])
        h = h + jnp.concatenate([y_conv, y_delta], axis=-1) @ w_out[l]
        u = rmsnorm(h, ffn_norm[l])
        h = h + hier_moe(u, w_group[l], b_group[l], w_router[l], b_router[l],
                         w_gate[l], w_up[l], w_down[l])
    return rmsnorm(h, final_norm)[:, N_META:]


_drawn_inputs = setup_inputs


def setup_inputs(seed=0):
    import zlib

    import numpy as np

    out = dict(_drawn_inputs(seed))
    spreads = {}
    factors = {'attn_norm': 3.403,
     'conv_ln_g': 12.531,
     'conv_ln_b': 24.536,
     'delta_norm_g': 3.714,
     'ffn_norm': 2.875,
     'b_group': 177.141,
     'b_router': 5.294,
     'final_norm': 21.144,
     'conv_dw_b': 3.368}
    for name, (base, spread) in spreads.items():
        noise = np.random.default_rng([zlib.crc32(name.encode()), seed]).standard_normal(out[name].shape)
        drawn = base * np.exp(spread * noise) if base else spread * noise
        out[name] = jnp.asarray(drawn.astype(out[name].dtype))
    for name, factor in factors.items():
        out[name] = (out[name] * factor).astype(out[name].dtype)
    return out
```

```python
from contextlib import ExitStack

import concourse.bass as bass
import numpy as np
from concourse import mybir

F32 = mybir.dt.float32
I32 = mybir.dt.int32
U32 = mybir.dt.uint32
ALU = mybir.AluOpType
ACT = mybir.ActivationFunctionType
AX = mybir.AxisListType.X

P = 128
D = 2048
KD = D // P
META = 16
SEQ = 256
TT = SEQ // P
T = META + SEQ
HD = 128
NH = 8
CW = 1024
TAPS = 31
SHORT = 4
QKV = 3 * NH
NG = 4
EPG = 8
NE = NG * EPG
FE = 512
KF = FE // P
CAP = 64
EPS = 1e-6
NEG = 3e38
SLOTS = 12
SLOT = 2048
BANK = 512
PAIRS = NE // 2
HISTORY = TAPS - 1 - META

C_ID, C_UP, C_LOW, C_SUP, C_ONE, C_I64, C_I32 = 0, 128, 256, 384, 512, 640, 768
C_END = 800
LEVELS = [1, 2, 4, 8, 16, 32, 64]

CHUNKS = [(0, META), (META, P), (META + P, P)]
GROUPS = [(c, hh) for c in range(3) for hh in range(2)]


def shape_constants():
    i, j = np.arange(P)[:, None], np.arange(P)[None, :]
    cst = np.zeros((P, C_END), np.float32)
    cst[:, C_ID:C_ID + P] = i == j
    cst[:, C_UP:C_UP + P] = i <= j
    cst[:, C_LOW:C_LOW + P] = i > j
    cst[:, C_SUP:C_SUP + P] = i < j
    cst[:, C_ONE:C_ONE + P] = 1
    cst[:, C_I64:C_I64 + P] = j % CAP
    cst[:, C_I32:C_I32 + NE] = np.arange(NE)
    masks = np.zeros((P, len(LEVELS), P), np.float32)
    for n, b in enumerate(LEVELS):
        masks[:, n] = (i // (2 * b) == j // (2 * b)) & (i // b % 2 == 1) & (j // b % 2 == 0)
    return cst, masks.reshape(P, -1)


def n_levels(c):
    return 4 if c == 0 else 7


def delta_events(engine, c):
    halves = [(f"a{v}", f"b{v}") for v in range(1, n_levels(c))]
    if engine == "pe":
        return ["turn", "decay", "lvl0"] + [x for h in halves for x in h] + ["solve", "apply"] + (["back"] if c else [])
    if engine == "act":
        return ["turn", "decay"] + [h[0] for h in halves] + ["solve"] + (["norm"] if c else [])
    if engine == "dve":
        return ["turn", "decay", "lvl0"] + [h[1] for h in halves] + ["apply"] + (["scale", "back"] if c else [])
    return [f"mask{v}" for v in range(n_levels(c))]


def delta_counts(engine):
    at, n = {}, 0
    for g in GROUPS:
        for e in delta_events(engine, g[0]):
            n += 1
            at[(g, e)] = n
    return at


PE_AT, ACT_AT, DVE_AT, POOL_AT = (delta_counts(e) for e in ("pe", "act", "dve", "pool"))

BLOCKS = [2048 + 512 * b for b in (2, 3, 4, 5, 0, 1)] + [5120, 5632, 1024, 0, 1536, 512]
QKV_ORDER = list(range(8, 24)) + list(range(8))
TAIL = [("z", j, 6 + j // 4, j % 4) for j in range(8)]
for j_ in range(8):
    TAIL += [("b", j_, 8 + 2 * (j_ // 4), j_ % 4), ("a", j_, 9 + 2 * (j_ // 4), j_ % 4)]
TILES_THROUGH = [4 * (b + 1) for b in range(6)] + [QKV + 1 + max(i for i, tl in enumerate(TAIL) if tl[2] == b)
                                                   for b in range(6, len(BLOCKS))]
K_ORDER = list(range(8, 16)) + list(range(8))
FREED = [(0 if s % 4 == 3 else len(BLOCKS) // 3) + (2 if s < 3 else 1) for s in range(SLOTS)]
N_PARAMS = 18
TAPS_BETWEEN = 3


def hybrid_kernel(nc, x, meta, attn_norm, w_in, conv_dw_w, conv_dw_b, conv_ln_g, conv_ln_b, short_conv_w,
                  a_log, dt_bias, delta_norm_g, w_out, ffn_norm, w_group, b_group, w_router, b_router,
                  w_gate, w_up, w_down, final_norm, cst_in, masks_in, out):
    with ExitStack() as ctx:
        def sb(name, cols, dt=F32):
            return ctx.enter_context(nc.sbuf_tensor(name, [P, cols], dt))

        def sem(name):
            return ctx.enter_context(nc.semaphore(name))

        ring = sb("ring", SLOTS * SLOT)
        region_h = sb("region_h", 4096)
        region_u = sb("region_u", KD * T)
        region_q = sb("region_q", QKV * (T + 3))
        region_y = sb("region_y", 8 * (HISTORY + T))
        region_s = sb("region_s", 1536)
        region_m = sb("region_m", 4096)
        cst = sb("cst", C_END)
        masks = sb("masks", len(LEVELS) * P)
        cols = sb("cols", 57 + 96 + 248)
        rows = sb("rows", 4 * P)
        w_ba = sb("w_ba", KD * 16)
        w_rt = sb("w_rt", KD * 36)
        conv_acc = sb("conv_acc", 2 * T)
        lmask1 = sb("lmask1", BANK)
        bias36 = sb("bias36", 36)
        dt_b = sb("dt_b", NH)
        alog_b = sb("alog_b", NH)
        small = sb("small", 512)
        rounds_i = sb("rounds_i", 1, I32)
        idx_u = sb("idx_u", 32, U32)
        rankm = sb("rankm", TT * 34)
        comb = sb("comb", TT * 34)
        banks = [ctx.enter_context(nc.psum_tensor(f"bank{i}", [P, BANK], F32))[:, :] for i in range(8)]

        slot = [ring[:, SLOT * s:SLOT * (s + 1)] for s in range(SLOTS)]
        ident, upper, lower = cst[:, C_ID:C_ID + P], cst[:, C_UP:C_UP + P], cst[:, C_LOW:C_LOW + P]
        supper, ones = cst[:, C_SUP:C_SUP + P], cst[:, C_ONE:C_ONE + P]
        mask3 = masks[:, :].rearrange("p (l n) -> p l n", n=P)
        g_attn, g_ffn, g_delta = cols[:, 0:16], cols[:, 16:32], cols[:, 32:33]
        short_w = cols[:, 57:153].rearrange("p (j c) -> p j c", c=QKV)
        dw_w = cols[:, 153:401].rearrange("p (j c) -> p j c", c=8)

        x_in = region_q[:, 0:4096].rearrange("p (t n) -> p t n", t=TT)
        m_in = region_m[0:META, 0:D]
        junk = region_u[:, 0:D]
        uT = region_u[:, 0:KD * T].rearrange("p (k t) -> p k t", t=T)
        raw = region_q[:, :].rearrange("p (c t) -> p c t", t=T + 3)
        glu = region_y[:, :].rearrange("p (c t) -> p c t", t=HISTORY + T)
        mixT = region_m[:, :].rearrange("p (c t) -> p c t", t=SEQ)

        def temp(n, base=region_h):
            return base[:, BANK * n:BANK * (n + 1)].rearrange("p (h n) -> p h n", h=4)
        k_tok, r_tok, scratch, decay, att, ug, x_inv, y_inv = (temp(n) for n in range(8))
        state = region_s[:, 0:1024].rearrange("p (h n) -> p h n", h=8)
        lmask = [temp(2, region_s), lmask1[:, :].rearrange("p (h n) -> p h n", h=4)]
        w_tok = lmask[1]
        o_tok = ug

        h_res = region_h[:, :].rearrange("p (t n) -> p t n", t=TT)
        un = region_u[:, 0:4096].rearrange("p (t n) -> p t n", t=TT)
        uTf = region_m[:, :].rearrange("p (k t) -> p k t", t=SEQ)
        uTe = region_q[:, 0:2048].rearrange("p (k n) -> p k n", n=P)
        baT = rows[0:16, 0:T]
        lgT = rows[0:36, 0:SEQ]
        ln_sq = [region_q[:, 2 * SEQ * i:2 * SEQ * (i + 1)].rearrange("p (c n) -> p c n", c=2) for i in range(4)]
        ypair = region_q[:, 4096:6144]
        hs = region_s[:, 0:512]
        hid = region_s[:, 512:1024]
        hidT = region_s[:, 1024:1536].rearrange("p (x k c) -> p x k c", x=2, c=CAP)
        sel_g = region_m[:, 0:256].rearrange("p (t n) -> p t n", t=TT)
        sel_w = region_m[:, 256:512].rearrange("p (t n) -> p t n", t=TT)
        sel_wT = region_m[:, 512:768]
        fin_g = region_m[:, 2048:4096]
        junk2 = region_y[:, 0:2048]

        ssq = small[:, 0:3]
        rstd = small[:, 3:6]
        ba_tok = small[:, 8:56].rearrange("p (c n) -> p c n", c=3)
        beta = small[:, 56:80].rearrange("p (c n) -> p c n", c=3)
        gdec = small[:, 80:104].rearrange("p (c n) -> p c n", c=3)
        ta = small[:, 104:128].rearrange("p (c n) -> p c n", c=3)
        tb = small[:, 128:152].rearrange("p (c n) -> p c n", c=3)
        ea = small[:, 152:160]
        egs = small[:, 160:232].rearrange("p (c n) -> p c n", c=3)
        kk, rk, qq, rq = (small[:, 232 + 4 * i:236 + 4 * i] for i in range(4))
        coef_s, coef_a, coef_b, coef_o = (small[:, 248 + 4 * i:252 + 4 * i] for i in range(4))
        oo, ro, rq2, lnt = (small[:, 264 + 4 * i:268 + 4 * i] for i in range(4))
        lnq = small[:, 280:284]
        logit = small[:, 0:72].rearrange("p (t n) -> p t n", t=TT)
        g8 = small[:, 72:88].rearrange("p (t n) -> p t n", t=TT)
        gm8 = small[:, 88:104].rearrange("p (t n) -> p t n", t=TT)
        gi = small[:, 104:120].rearrange("p (t n) -> p t n", t=TT)
        goh = small[:, 120:128].rearrange("p (t n) -> p t n", t=TT)
        gneg = small[:, 128:136].rearrange("p (t n) -> p t n", t=TT)
        gex = small[:, 136:144].rearrange("p (t n) -> p t n", t=TT)
        pg = small[:, 144:146]
        ngm = small[:, 146:148]
        es = small[:, 148:212].rearrange("p (t n) -> p t n", t=TT)
        ev = small[:, 212:228].rearrange("p (t n) -> p t n", t=TT)
        ei = small[:, 228:244].rearrange("p (t n) -> p t n", t=TT)
        dv = small[:, 244:246]
        ex = small[:, 246:248]
        w1 = small[:, 248:250]
        w2 = small[:, 250:252]
        oh1 = small[:, 252:316].rearrange("p (t n) -> p t n", t=TT)
        oh2 = small[:, 316:380].rearrange("p (t n) -> p t n", t=TT)
        cmx = small[:, 380:381]
        rnd = small[:, 381:384]
        ssh = small[:, 384:386]
        rsh = small[:, 386:388]
        idx3 = idx_u[:, :].rearrange("p (a t n) -> p a t n", a=2, t=TT)
        rank3 = rankm[:, :].rearrange("p (t n) -> p t n", t=TT)
        comb3 = comb[:, :].rearrange("p (t n) -> p t n", t=TT)

        slot_full = [sem(f"slot_full{s}") for s in range(SLOTS)]
        slot_free = [sem(f"slot_free{s}") for s in range(SLOTS)]
        x_loaded0 = sem("x_loaded0")
        x_loaded1 = sem("x_loaded1")
        x_loaded2 = sem("x_loaded2")
        params_loaded = sem("params_loaded")
        h_loaded = sem("h_loaded")
        fin_loaded = sem("fin_loaded")
        out_stored = sem("out_stored")
        zeroed = sem("zeroed")
        squares_done = sem("squares_done")
        x_normed = sem("x_normed")
        x_turned = sem("x_turned")
        ut_dve = sem("ut_dve")
        ut_act = sem("ut_act")
        cols_turned = sem("cols_turned")
        cols_ready = sem("cols_ready")
        ba_done = sem("ba_done")
        ba_copied = sem("ba_copied")
        ba_turned = sem("ba_turned")
        gate_act = sem("gate_act")
        gate_dve = sem("gate_dve")
        gsum_done = sem("gsum_done")
        gexp_ready = sem("gexp_ready")
        tile_done = sem("tile_done")
        tile_read0 = sem("tile_read0")
        tile_read1 = sem("tile_read1")
        raw_copied = sem("raw_copied")
        short_done = sem("short_done")
        silu_done = sem("silu_done")
        gate_exp = sem("gate_exp")
        gated = sem("gated")
        conv_tap = sem("conv_tap")
        delta_pe = sem("delta_pe")
        delta_act = sem("delta_act")
        delta_dve = sem("delta_dve")
        delta_pool = sem("delta_pool")
        ln_pe = sem("ln_pe")
        ln_dve = sem("ln_dve")
        ln_act = sem("ln_act")
        mix_done = sem("mix_done")
        out_done = sem("out_done")
        h_ready = sem("h_ready")
        h_rstd = sem("h_rstd")
        un_ready = sem("un_ready")
        un_turned = sem("un_turned")
        utf_ready = sem("utf_ready")
        logits_done = sem("logits_done")
        logits_copied = sem("logits_copied")
        logits_turned = sem("logits_turned")
        route_dve = sem("route_dve")
        route_act = sem("route_act")
        route_pe = sem("route_pe")
        route_first = sem("route_first")
        route_second = sem("route_second")
        next_ranks = sem("next_ranks")
        plan_ready = sem("plan_ready")
        sel_ready = sem("sel_ready")
        gather_done = sem("gather_done")
        gather_read = sem("gather_read")
        scatter_done = sem("scatter_done")
        scatter_read = sem("scatter_read")
        selw_turned = sem("selw_turned")
        selw_ready = sem("selw_ready")
        gu_done = sem("gu_done")
        silu_gate = sem("silu_gate")
        hid_ready = sem("hid_ready")
        hid_turned = sem("hid_turned")
        hidt_ready = sem("hidt_ready")
        down_done = sem("down_done")
        y_act = sem("y_act")
        y_dve = sem("y_dve")
        order_dve = sem("order_dve")
        order_act = sem("order_act")
        acc_done = sem("acc_done")
        fin_act = sem("fin_act")
        fin_dve = sem("fin_dve")

        class Order:

            def __init__(self, eng, s):
                self.eng, self.s, self.n, self.base = eng, s, 0, 0

            def then(self, ins):
                ins.then_inc(self.s, 1)
                self.n += 1
                return ins

            def settle(self):
                self.eng.wait_ge(self.s, self.base + self.n)

        def slot_uses(s):
            return len(BLOCKS) // 3 + (KD + SLOTS - 1 - s) // SLOTS

        def b4(ap, n=P):
            return ap.unsqueeze(2).to_broadcast([ap.shape[0], 4, n])

        def m4(ap):
            return ap.unsqueeze(1).to_broadcast([ap.shape[0], 4, ap.shape[1]])

        bk = [b_[:, :].rearrange("p (h n) -> p h n", h=4) for b_ in banks]
        lnh = small[:, 388:389]
        block = ctx.enter_context(nc.Block())

        w_in_v = w_in[0].rearrange("(k p) n -> p k n", p=P)
        w_out_v = w_out[0].rearrange("(k p) n -> k p n", p=P)
        gate_v = w_gate[0].rearrange("e (g k p) n -> e g p k n", p=P, k=4)
        up_v = w_up[0].rearrange("e (g k p) n -> e g p k n", p=P, k=4)
        down_v = w_down[0].rearrange("e (k p) n -> e k p n", p=P)
        x_v = x[0].rearrange("(t p) n -> p t n", p=P)
        out_v = out[0].rearrange("(t p) n -> p t n", p=P)

        def read_rounds(eng):
            eng.wait_ge(plan_ready, 1)
            return eng.value_load(rounds_i[0:1, 0:1], min_val=1, max_val=SEQ // CAP)

        @block.sync
        def _(sp):
            sp.dma_start(m_in, meta).then_inc(x_loaded2, 16)
            sp.dma_start(x_in[:, 0, :], x_v[:, 0, :]).then_inc(x_loaded0, 16)
            sp.dma_start(x_in[:, 1, :], x_v[:, 1, :]).then_inc(x_loaded1, 16)
            for b in range(len(BLOCKS)):
                for g in range(4):
                    s = 4 * (b % 3) + g
                    if b >= 3 and g < 3:
                        sp.wait_ge(slot_free[s], b // 3)
                    elif b >= 3:
                        sp.wait_ge(tile_done, TILES_THROUGH[b - 3])
                    sp.dma_start(slot[s].rearrange("p (k n) -> p k n", k=4),
                                 w_in_v[:, 4 * g:4 * g + 4, BLOCKS[b]:BLOCKS[b] + 512]).then_inc(slot_full[s], 16)
            for n, k in enumerate(K_ORDER):
                s = n % SLOTS
                if n >= SLOTS:
                    sp.wait_ge(slot_free[s], FREED[s] - (s < 3))
                elif s % 4 < 3:
                    sp.wait_ge(slot_free[s], len(BLOCKS) // 3)
                else:
                    sp.wait_ge(tile_done, TILES_THROUGH[len(BLOCKS) - 3 + s // 4])
                sp.dma_start(slot[s], w_out_v[k]).then_inc(slot_full[s], 16)
                if n == SLOTS - 1:
                    sp.wait_ge(delta_dve, DVE_AT[(GROUPS[-1], "back")])
                    sp.dma_start(h_res, x_v).then_inc(h_loaded, 16)

            def load_expert(e, u):
                first = isinstance(u, int) and u == 0
                order = [(4 * v + g, (gate_v, up_v)[v], g) for g in range(4) for v in range(2)]
                order += [(8 + k, down_v, k) for k in range(KF)]
                for s, view, g in order:
                    if first and s == 3:
                        sp.wait_ge(out_done, 2)
                    elif s == 7 and not first:
                        sp.wait_ge(gu_done, u)
                    elif s == 11 and not first:
                        sp.wait_ge(down_done, u)
                    else:
                        sp.wait_ge(slot_free[s], u + (1 if s in (7, 11) else FREED[s]))
                    src = view[e, g]
                    dst = slot[s] if s >= 8 else slot[s].rearrange("p (k n) -> p k n", k=4)
                    sp.dma_start(dst, src).then_inc(slot_full[s], 16)
            load_expert(0, 0)
            sp.wait_ge(plan_ready, 1)
            sp.dma_start(fin_g, final_norm.partition_broadcast(P)).then_inc(fin_loaded, 16)
            with sp.Fori(1, NE) as e:
                load_expert(e, e)
            rounds = read_rounds(sp)
            with sp.If(rounds > 1):
                with sp.Fori(1, rounds) as r:
                    with sp.Fori(0, NE) as e:
                        load_expert(e, r * NE + e)
            for t in range(TT):
                sp.wait_ge(fin_dve, t + 1)
                sp.dma_start(out_v[:, t, :], un[:, t, :]).then_inc(out_stored, 16)
            sp.wait_ge(out_stored, 16 * TT)

        @block.tensor
        def _(pe):
            mm, tr = nc.tensor.matmul, nc.tensor.transpose
            pe.wait_ge(params_loaded, 16 * N_PARAMS)
            for i, (n, at) in enumerate(((57, 0), (96, 57), (124, 153), (124, 277))):
                last = tr(banks[7][:, at:at + n], rows[0:n, P * i:P * (i + 1)], ident[0:n, 0:n])
            last.then_inc(cols_turned, 1)
            pe.wait_ge(x_normed, 3)
            for k in range(KD):
                if k >= 4:
                    pe.wait_ge(ut_act if k % 2 else ut_dve, (k - 4) // 2 + 1)
                b = banks[k % 4]
                tr(b[:, 0:META], m_in[:, P * k:P * (k + 1)], ident[0:META, 0:META])
                for t in range(TT):
                    last = tr(b[:, META + P * t:META + P * (t + 1)], x_in[:, t, P * k:P * (k + 1)], ident)
                last.then_inc(x_turned, 1)
            pe.wait_ge(ut_act, KD // 2)
            pe.wait_ge(ut_dve, KD // 2)
            for k in range(KD):
                last = mm(banks[4][0:16, 0:T], w_ba[:, 16 * k:16 * (k + 1)], uT[:, k, :], start=k == 0, stop=k == KD - 1)
            last.then_inc(ba_done, 1)

            def project(n, b, j, width):
                if n >= 2:
                    pe.wait_ge((tile_read0, tile_read1)[n % 2], n // 2)
                for g in range(4):
                    s = 4 * (b % 3) + g
                    pe.wait_ge(slot_full[s], 16 * (b // 3 + 1))
                    for k in range(4):
                        last = mm(banks[n % 2][:, 0:width], slot[s][:, 512 * k + P * j:512 * k + P * (j + 1)],
                                  uT[:, 4 * g + k, T - width:T], start=g == k == 0, stop=g == k == 3)
                    if g == 3:
                        last.then_inc(tile_done, 1)
                    elif j == 3:
                        last.then_inc(slot_free[s], 1)
                    yield

            n = 0
            for b in range(6):
                for j in range(4):
                    for _ in project(n, b, j, T):
                        pass
                    n += 1
                    if n == 1:
                        pe.wait_ge(ba_copied, 1)
                        for c, (t0, m) in enumerate(CHUNKS):
                            last = tr(banks[5][0:m, 16 * c:16 * (c + 1)], baT[:, t0:t0 + m], ident[0:16, 0:16])
                        last.then_inc(ba_turned, 1)
                    if n == 3:
                        pe.wait_ge(gate_dve, 6)
                        for c, (t0, m) in enumerate(CHUNKS):
                            o = 24 * c
                            mm(banks[6][0:m, o:o + 8], upper[0:m, 0:m], gdec[0:m, c, :], start=True, stop=True)
                            mm(banks[6][0:m, o + 8:o + 16], lower[0:m, 0:m], gdec[0:m, c, :], start=True, stop=True)
                            last = mm(banks[6][:, o + 16:o + 24], ones[0:m, :], gdec[0:m, c, :], start=True, stop=True)
                        last.then_inc(gsum_done, 1)

            def delta():
                pe.wait_ge(silu_done, QKV)
                pe.wait_ge(gexp_ready, 9)
                prev = None
                for g in GROUPS:
                    c, hh = g
                    t0, m = CHUNKS[c]
                    heads = [(j, 4 * hh + j) for j in range(4)]
                    q_, k_, v_ = (lambda h, o=o: raw[:, o + h, SHORT - 1 + t0:SHORT - 1 + t0 + m] for o in (0, 8, 16))
                    if prev:
                        pe.wait_ge(delta_dve, DVE_AT[(prev, delta_events("dve", prev[0])[-1])])
                        pe.wait_ge(delta_act, ACT_AT[(prev, delta_events("act", prev[0])[-1])])
                    for j, h in heads:
                        tr(bk[2][0:m, j, :], k_(h), ident)
                        tr(bk[3][0:m, j, :], v_(h), ident)
                        if c:
                            tr(bk[4][0:m, j, :], q_(h), ident)
                        last = mm(bk[5][0:m, j, 0:m], k_(h), k_(h), start=True, stop=True)
                    last.then_inc(delta_pe, 1)
                    yield
                    pe.wait_ge(delta_dve, DVE_AT[(g, "turn")])
                    pe.wait_ge(delta_act, ACT_AT[(g, "turn")])
                    for j, h in heads:
                        last = mm(bk[6][0:m, j, 0:m], ug[0:m, j, 0:m], lower[0:m, 0:m], start=True, stop=True)
                    if c:
                        mm(banks[7][0:m, :], lower[0:m, 0:m], ug[0:m, :, 0:m], start=True, stop=True)
                        for j, h in heads:
                            last = mm(bk[2][0:m, j, 0:m], k_(h), q_(h), start=True, stop=True)
                    last.then_inc(delta_pe, 1)
                    yield
                    pe.wait_ge(delta_pool, POOL_AT[(g, "mask0")])
                    for j, h in heads:
                        last = tr(bk[3][0:m, j, 0:m], lmask[0][0:m, j, 0:m], ident[0:m, 0:m])
                    if c:
                        for j, h in heads:
                            mm(bk[5][:, j, :], k_(h), state[:, h, :], start=True, stop=True)
                            last = mm(bk[2][:, j, :], q_(h), state[:, h, :], start=True, stop=True)
                    last.then_inc(delta_pe, 1)
                    yield
                    for v in range(1, n_levels(c)):
                        pe.wait_ge(delta_pool, POOL_AT[(g, f"mask{v}")])
                        pe.wait_ge(delta_dve, DVE_AT[(g, "lvl0" if v == 1 else f"b{v - 1}")])
                        for j, h in heads:
                            last = mm(bk[3][0:m, j, 0:m], lmask[v % 2][0:m, j, 0:m], y_inv[0:m, j, 0:m],
                                      start=True, stop=True)
                        last.then_inc(delta_pe, 1)
                        yield
                        pe.wait_ge(delta_act, ACT_AT[(g, f"a{v}")])
                        for j, h in heads:
                            last = mm(bk[4][0:m, j, 0:m], x_inv[0:m, j, 0:m], scratch[0:m, j, 0:m], start=True, stop=True)
                            if v < n_levels(c) - 1:
                                last = mm(bk[6][0:m, j, 0:m], scratch[0:m, j, 0:m], x_inv[0:m, j, 0:m],
                                          start=True, stop=True)
                        last.then_inc(delta_pe, 1)
                        yield
                    pe.wait_ge(delta_dve, DVE_AT[(g, f"b{n_levels(c) - 1}")])
                    for j, h in heads:
                        last = mm(bk[7][0:m, j, :], y_inv[0:m, j, 0:m], r_tok[0:m, j, :], start=True, stop=True)
                    last.then_inc(delta_pe, 1)
                    yield
                    pe.wait_ge(delta_act, ACT_AT[(g, "solve")])
                    for j, h in heads:
                        if c < 2:
                            last = mm(bk[6][:, j, :], k_tok[0:m, j, :], w_tok[0:m, j, :], start=True, stop=True)
                        if c:
                            last = mm(bk[4][:, j, :], att[0:m, j, 0:m], w_tok[0:m, j, :], start=True, stop=True)
                    last.then_inc(delta_pe, 1)
                    yield
                    if c:
                        pe.wait_ge(delta_dve, DVE_AT[(g, "scale")])
                        for j, h in heads:
                            last = tr(bk[3][:, j, :], o_tok[:, j, :], ident)
                        last.then_inc(delta_pe, 1)
                        yield
                    prev = g

            steps = delta()
            for kind, _, b, j in TAIL:
                for _ in project(n, b, j, SEQ if kind == "z" else T):
                    next(steps, None)
                n += 1
            for _ in steps:
                pass

            pe.wait_ge(delta_dve, DVE_AT[(GROUPS[-1], "back")])
            pe.wait_ge(tile_read0, n // 2)
            pe.wait_ge(tile_read1, n // 2)
            for i in range(4):
                pe.wait_ge(conv_tap, 2 * TAPS * (i + 1))
                mm(banks[i], ones, mixT[:, 2 * i:2 * i + 2, :], start=True, stop=True).then_inc(ln_pe, 1)
            for i in range(4):
                pe.wait_ge(ln_act, i + 1)
                mm(banks[4 + i], ones, ln_sq[i], start=True, stop=True).then_inc(ln_pe, 1)

            pe.wait_ge(ln_dve, 4)
            pe.wait_ge(ln_act, 8)
            for n_k, k in enumerate(K_ORDER):
                s = n_k % SLOTS
                pe.wait_ge(slot_full[s], 16 * (len(BLOCKS) // 3 + n_k // SLOTS + 1))
                if k < 8 and k % 2 == 0:
                    pe.wait_ge(mix_done, k // 2 + 1)
                for t in range(TT):
                    for q in range(4):
                        last = mm(banks[4 * t + q], mixT[:, k, P * t:P * (t + 1)], slot[s][:, BANK * q:BANK * (q + 1)],
                                  start=n_k == 0, stop=n_k == KD - 1)
                    if n_k == KD - 1:
                        last.then_inc(out_done, 1)
                if n_k < KD - 1:
                    last.then_inc(slot_free[s], 1)

            for t in range(TT):
                pe.wait_ge(un_ready, t + 1)
                for g in range(4):
                    i = 4 * t + g
                    if i >= 4:
                        pe.wait_ge(utf_ready, i - 3)
                    for k in range(4):
                        last = tr(banks[i % 4][:, P * k:P * (k + 1)], un[:, t, P * (4 * g + k):P * (4 * g + k + 1)], ident)
                    last.then_inc(un_turned, 1)
            pe.wait_ge(utf_ready, 8)
            for k in range(KD):
                last = mm(banks[4][0:36, 0:SEQ], w_rt[:, 36 * k:36 * (k + 1)], uTf[:, k, :], start=k == 0, stop=k == KD - 1)
            last.then_inc(logits_done, 1)
            pe.wait_ge(logits_copied, 1)
            for t in range(TT):
                last = tr(banks[5][:, 36 * t:36 * (t + 1)], lgT[:, P * t:P * (t + 1)], ident[0:36, 0:36])
            last.then_inc(logits_turned, 1)
            pe.wait_ge(route_dve, 1)
            mm(banks[6][:, 0:NE], supper, oh1[:, 0, :], start=True, stop=True)
            mm(banks[6][:, NE:2 * NE], supper, oh1[:, 1, :], start=True, stop=False)
            mm(banks[6][:, NE:2 * NE], ones, oh1[:, 0, :], start=False, stop=True)
            mm(banks[6][:, 2 * NE:3 * NE], ones, oh1[:, 0, :], start=True, stop=False)
            mm(banks[6][:, 2 * NE:3 * NE], ones, oh1[:, 1, :], start=False, stop=True).then_inc(route_pe, 1)

            def gather(p):
                pe.wait_ge(sel_ready, p + 1)
                for g in range(4):
                    if not isinstance(p, int) or p > 0 or g >= 2:
                        pe.wait_ge(gather_read, 4 * p + g - 1)
                    for k in range(4):
                        c0 = P * (4 * g + k)
                        for t in range(TT):
                            last = mm(banks[5 + g % 2][:, P * k:P * (k + 1)], un[:, t, c0:c0 + P], sel_g[:, t, :],
                                      start=t == 0, stop=t == TT - 1)
                    last.then_inc(gather_done, 1)

            def turn_weights(p):
                if not isinstance(p, int) or p > 0:
                    pe.wait_ge(scatter_read, 8 * p)
                for t in range(TT):
                    last = tr(banks[7][:, P * t:P * (t + 1)], sel_w[:, t, :], ident)
                last.then_inc(selw_turned, 1)

            def full(s, u):
                pe.wait_ge(slot_full[s], 16 * (u + slot_uses(s) + 1))

            def gate_up(u, x_):
                if not isinstance(u, int) or u >= 2:
                    pe.wait_ge(hid_ready, u - 1)
                for g in range(4):
                    full(g, u)
                    full(4 + g, u)
                    for k in range(4):
                        for v in range(2):
                            last = mm(banks[x_][CAP * v:CAP * (v + 1), :], uTe[:, 4 * g + k, CAP * x_:CAP * (x_ + 1)],
                                      slot[4 * v + g][:, 512 * k:512 * (k + 1)], start=g == k == 0, stop=g == k == 3)
                            if k == 3 and v == 1 and g == 3:
                                last.then_inc(gu_done, 1)
                            elif k == 3:
                                last.then_inc(slot_free[4 * v + g], 1)

            def down(u, x_):
                pe.wait_ge(hid_ready, u + 1)
                for f in range(KF):
                    last = tr(banks[2][:, P * f:P * (f + 1)], hid[:, P * f:P * (f + 1)], ident)
                last.then_inc(hid_turned, 1)
                pe.wait_ge(hidt_ready, u + 1)
                if not isinstance(u, int) or u > 0:
                    pe.wait_ge(y_act, u)
                    pe.wait_ge(y_dve, u)
                for f in range(KF):
                    full(8 + f, u)
                    for q in range(2):
                        for v in range(2):
                            c0 = 1024 * v + BANK * q
                            last = mm(banks[3 + q][CAP * v:CAP * (v + 1), :], hidT[:, x_, f, :],
                                      slot[8 + f][:, c0:c0 + BANK], start=f == 0, stop=f == KF - 1)
                    last.then_inc(slot_free[8 + f] if f < KF - 1 else down_done, 1)

            def scatter(p):
                pe.wait_ge(selw_ready, p + 1)
                pe.wait_ge(y_act, 2 * p + 2)
                pe.wait_ge(y_dve, 2 * p + 2)
                for i in range(8):
                    if i >= 2:
                        pe.wait_ge(scatter_read, 8 * p + i - 1)
                    mm(banks[7 if i % 2 else 2], sel_wT[:, P * (i // 4):P * (i // 4 + 1)],
                       ypair[:, BANK * (i % 4):BANK * (i % 4 + 1)], start=True, stop=True).then_inc(scatter_done, 1)

            def pair(p, last_pair):
                pe.wait_ge(gather_read, 4 * p + 4)
                gate_up(2 * p, 0)
                turn_weights(p)
                down(2 * p, 0)
                gate_up(2 * p + 1, 1)
                if not last_pair:
                    gather(p + 1)
                down(2 * p + 1, 1)
                scatter(p)

            def one_round(r):
                gather(r * PAIRS)
                first = isinstance(r, int)
                if first:
                    pair(0, False)
                with pe.Fori(1 if first else 0, PAIRS - 1) as i:
                    pair(r * PAIRS + i, False)
                pair(r * PAIRS + PAIRS - 1, True)
            pe.wait_ge(plan_ready, 1)
            one_round(0)
            rounds = read_rounds(pe)
            with pe.If(rounds > 1):
                with pe.Fori(1, rounds) as r:
                    one_round(r)

        @block.scalar
        def _(act):
            act_fn = nc.scalar.activation
            own = Order(act, order_act)

            def rsqrt(out_, in_, scale, last_sem=None):
                own.then(act_fn(lnt_of(out_), in_, ACT.Ln, bias=EPS, scale=scale))
                own.settle()
                return act_fn(out_, lnt_of(out_), ACT.Exp, scale=-0.5)

            def lnt_of(out_):
                n = out_.shape[-1]
                return lnt[0:out_.shape[0], 0:n]

            rows_of = ((attn_norm, 0), (ffn_norm, 16), (delta_norm_g, 32), (conv_dw_b, 33), (conv_ln_g, 41), (conv_ln_b, 49))
            loads = [(rows[r:r + a.shape[1] // P, 0:P], a[0].rearrange("(r n) -> r n", n=P)) for a, r in rows_of]
            loads.append((rows[0:96, P:2 * P], short_conv_w[0].rearrange("j (c n) -> (j c) n", n=P)))
            dw = conv_dw_w[0].rearrange("j (c n) -> (j c) n", n=P)
            loads += [(rows[0:124, P * (2 + i):P * (3 + i)], dw[124 * i:124 * (i + 1), :]) for i in range(2)]
            w_rt3 = w_rt[:, :].rearrange("p (k n) -> p k n", k=KD)
            loads += [(cst[:, :], cst_in), (masks[:, :], masks_in),
                      (w_ba[:, :].rearrange("p (k n) -> p k n", k=KD), w_in[0, :, 6144:6160].rearrange("(k p) n -> p k n", p=P)),
                      (w_rt3[:, :, 0:NG], w_group[0].rearrange("(k p) n -> p k n", p=P)),
                      (w_rt3[:, :, NG:], w_router[0].rearrange("(k p) n -> p k n", p=P)),
                      (bias36[:, 0:NG], b_group[0, :].partition_broadcast(P)),
                      (bias36[:, NG:], b_router[0, :].partition_broadcast(P)),
                      (dt_b[:, :], dt_bias[0, :].partition_broadcast(P)),
                      (alog_b[:, :], a_log[0, :].partition_broadcast(P))]
            assert len(loads) == N_PARAMS
            for dst, src in loads:
                act.dma_start(dst, src).then_inc(params_loaded, 16)

            parts = ((x_in[:, 0, :], x_loaded0, P), (x_in[:, 1, :], x_loaded1, P), (m_in, x_loaded2, META))
            for i, (v, loaded, m) in enumerate(parts):
                act.wait_ge(loaded, 16)
                own.then(act_fn(junk[0:m], v, ACT.Square, accum_out=ssq[0:m, i:i + 1]))
                own.settle()
                own.then(rsqrt(rstd[0:m, i:i + 1], ssq[0:m, i:i + 1], 1.0 / D))
                own.settle()
                act_fn(v, v, ACT.Copy, scale=rstd[0:m, i:i + 1]).then_inc(x_normed, 1)
            act.wait_ge(cols_ready, 1)
            for k in range(1, KD, 2):
                act.wait_ge(x_turned, k + 1)
                act_fn(uT[:, k, :], banks[k % 4][:, 0:T], ACT.Copy, scale=g_attn[:, k:k + 1]).then_inc(ut_act, 1)

            def take_raw(n):
                act.wait_ge(tile_done, n + 1)
                if n == 0:
                    act.wait_ge(zeroed, 3)
                act_fn(raw[:, QKV_ORDER[n], SHORT - 1:], banks[n % 2][:, 0:T], ACT.Copy).then_inc(
                    (tile_read0, tile_read1)[n % 2], 1)

            def silu_raw(n):
                act.wait_ge(short_done, n + 1)
                act_fn(raw[:, QKV_ORDER[n], SHORT - 1:], conv_acc[:, T * (n % 2):T * (n % 2 + 1)], ACT.Silu
                       ).then_inc(silu_done, 1)

            def gate_logits():
                act.wait_ge(gate_dve, 2)
                act_fn(tb[:, :, :], ta[:, :, :], ACT.Exp, scale=-1.0).then_inc(gate_act, 1)
                act_fn(beta[:, :, :], ba_tok[:, :, 0:NH], ACT.Exp, scale=-1.0).then_inc(gate_act, 1)
                act.wait_ge(params_loaded, 16 * N_PARAMS)
                act_fn(ea, alog_b[:, :], ACT.Exp).then_inc(gate_act, 1)
                act.wait_ge(gate_act, 1)
                act_fn(ta[:, :, :], tb[:, :, :], ACT.Ln, bias=1.0).then_inc(gate_act, 1)

            def decays():
                act.wait_ge(gsum_done, 1)
                for c, (_, m) in enumerate(CHUNKS):
                    for at, n_ in ((0, m), (8, m), (16, P)):
                        act_fn(egs[0:n_, c, at:at + 8], banks[6][0:n_, 24 * c + at:24 * c + at + 8], ACT.Exp
                               ).then_inc(gexp_ready, 1)

            for n in range(QKV + 1):
                if n < QKV:
                    take_raw(n)
                if n == 0:
                    gate_logits()
                if n == 4:
                    decays()
                if n >= 1:
                    silu_raw(n - 1)

            def delta():
                for g in GROUPS:
                    c, hh = g
                    t0, m = CHUNKS[c]
                    act.wait_ge(delta_pe, PE_AT[(g, "turn")])
                    act_fn(k_tok[0:m], bk[2][0:m], ACT.Copy)
                    act_fn(r_tok[0:m], bk[3][0:m], ACT.Copy)
                    last = act_fn(scratch[0:m], bk[2][0:m], ACT.Square)
                    if c:
                        last = act_fn(x_inv[0:m], bk[4][0:m], ACT.Square)
                    last.then_inc(delta_act, 1)
                    yield
                    act.wait_ge(delta_dve, DVE_AT[(g, "turn")])
                    own.then(act_fn(lnt[0:m], kk[0:m], ACT.Ln, bias=EPS))
                    if c:
                        own.then(act_fn(lnq[0:m], qq[0:m], ACT.Ln, bias=EPS))
                    own.settle()
                    own.then(act_fn(rk[0:m], lnt[0:m], ACT.Exp, scale=-0.5))
                    if c:
                        own.then(act_fn(rq[0:m], lnq[0:m], ACT.Exp, scale=-0.5))
                        own.then(act_fn(rq2[0:m], lnq[0:m], ACT.Exp, scale=-1.0))
                    act.wait_ge(delta_pe, PE_AT[(g, "decay")])
                    last = act_fn(decay[0:m, :, 0:m], bk[6][0:m, :, 0:m], ACT.Exp)
                    if c:
                        last = act_fn(att[0:m, :, 0:m], bk[7][0:m, :, 0:m], ACT.Exp)
                    last.then_inc(delta_act, 1)
                    yield
                    yield
                    for v in range(1, n_levels(c)):
                        act.wait_ge(delta_pe, PE_AT[(g, f"a{v}")])
                        act_fn(scratch[0:m, :, 0:m], bk[3][0:m, :, 0:m], ACT.Copy).then_inc(delta_act, 1)
                        yield
                        yield
                    act.wait_ge(delta_pe, PE_AT[(g, "solve")])
                    act_fn(w_tok[0:m], bk[7][0:m], ACT.Copy).then_inc(delta_act, 1)
                    yield
                    if c:
                        act.wait_ge(delta_dve, DVE_AT[(g, "apply")])
                        own.then(act_fn(lnt[0:m], oo[0:m], ACT.Ln, bias=EPS))
                        own.settle()
                        act_fn(ro[0:m], lnt[0:m], ACT.Exp, scale=-0.5).then_inc(delta_act, 1)
                    yield
                    if c:
                        yield

            def gate(n, m):
                act.wait_ge(tile_done, n + 1)
                if m >= 2:
                    act.wait_ge(gated, m - 1)
                width = SEQ if m < 8 else T
                return act_fn(conv_acc[:, T * (m % 2):T * (m % 2) + width], banks[n % 2][:, 0:width], ACT.Exp, scale=-1.0)

            steps = delta()
            for i, (kind, j, _, _) in enumerate(TAIL):
                for _ in range(4):
                    next(steps, None)
                n = QKV + i
                if kind == "z":
                    gate(n, j).then_inc(gate_exp, 1)
                elif kind == "b":
                    gate(n, 8 + j).then_inc((tile_read0, tile_read1)[n % 2], 1)
            for _ in steps:
                pass

            for i in range(4):
                act.wait_ge(ln_dve, i + 1)
                act_fn(ln_sq[i], mixT[:, 2 * i:2 * i + 2, :], ACT.Square).then_inc(ln_act, 1)
            for i in range(4):
                act.wait_ge(ln_pe, 5 + i)
                own.then(act_fn(ln_sq[i], banks[4 + i][:, :].rearrange("p (c n) -> p c n", c=2), ACT.Ln, bias=EPS,
                                scale=1.0 / P))
                own.settle()
                act_fn(ln_sq[i], ln_sq[i], ACT.Exp, scale=-0.5).then_inc(ln_act, 1)
            for i in range(4):
                act.wait_ge(ln_dve, 5 + i)
                act_fn(mixT[:, 2 * i:2 * i + 2, :], mixT[:, 2 * i:2 * i + 2, :], ACT.Silu).then_inc(mix_done, 1)

            for t in range(TT):
                act.wait_ge(h_ready, t + 1)
                own.then(act_fn(junk2, h_res[:, t, :], ACT.Square, accum_out=ssh[:, t:t + 1]))
                own.settle()
                own.then(act_fn(lnh, ssh[:, t:t + 1], ACT.Ln, bias=EPS, scale=1.0 / D))
                own.settle()
                act_fn(rsh[:, t:t + 1], lnh, ACT.Exp, scale=-0.5).then_inc(h_rstd, 1)
            act.wait_ge(logits_done, 1)
            act_fn(lgT, banks[4][0:36, 0:SEQ], ACT.Copy).then_inc(logits_copied, 1)
            act.wait_ge(route_first, 1)
            for t in range(TT):
                act_fn(gex[:, t, :], logit[:, t, 0:NG], ACT.Exp, bias=ngm[:, t:t + 1], accum_out=pg[:, t:t + 1]
                       ).then_inc(route_act, 1)
            act.wait_ge(route_second, 1)
            act_fn(ex, dv, ACT.Exp).then_inc(route_act, 1)

            def expert(p, x_):
                u = 2 * p + x_
                act.wait_ge(gu_done, u + 1)
                if not isinstance(u, int) or u > 0:
                    act.wait_ge(hid_ready, u)
                act_fn(hs[CAP:P, :], banks[x_][0:CAP, :], ACT.Silu).then_inc(silu_gate, 1)
                if x_ == 0:
                    act.wait_ge(selw_turned, p + 1)
                    act_fn(sel_wT, banks[7][:, 0:SEQ], ACT.Copy).then_inc(selw_ready, 1)
                act.wait_ge(hid_turned, u + 1)
                act_fn(hidT[:, x_], banks[2][:, :].rearrange("p (k n) -> p k n", k=KF)[:, :, CAP:P], ACT.Copy
                       ).then_inc(hidt_ready, 1)
                act.wait_ge(down_done, u + 1)
                for v in range(2):
                    c0 = 1024 * v + BANK
                    last = act_fn(ypair[CAP * x_:CAP * (x_ + 1), c0:c0 + BANK], banks[4][CAP * v:CAP * (v + 1), :], ACT.Copy)
                last.then_inc(y_act, 1)

            def pair(p):
                expert(p, 0)
                expert(p, 1)

            act.wait_ge(plan_ready, 1)
            pair(0)
            with act.Fori(1, PAIRS) as i:
                pair(i)
            rounds = read_rounds(act)
            with act.If(rounds > 1):
                with act.Fori(1, rounds) as r:
                    with act.Fori(0, PAIRS) as i:
                        pair(r * PAIRS + i)
            act.wait_ge(acc_done, 1)
            for t in range(TT):
                own.then(act_fn(junk2, h_res[:, t, :], ACT.Square, accum_out=ssh[:, t:t + 1]))
                own.settle()
                own.then(act_fn(lnh, ssh[:, t:t + 1], ACT.Ln, bias=EPS, scale=1.0 / D))
                own.settle()
                act_fn(rsh[:, t:t + 1], lnh, ACT.Exp, scale=-0.5).then_inc(fin_act, 1)

        @block.vector
        def _(dve):
            tt, ts, stt = dve.tensor_tensor, dve.tensor_scalar, dve.scalar_tensor_tensor
            own = Order(dve, order_dve)

            def step(ins):
                own.then(ins)
                own.settle()

            dve.wait_ge(cols_turned, 1)
            dve.tensor_copy(cols[:, 0:57], banks[7][:, 0:57])
            dve.tensor_copy(cols[:, 57:153], banks[7][:, 57:153])
            dve.tensor_copy(cols[:, 153:401], banks[7][:, 153:401]).then_inc(cols_ready, 1)
            dve.wait_ge(cols_ready, 1)
            for k in range(0, KD, 2):
                dve.wait_ge(x_turned, k + 1)
                ts(uT[:, k, :], banks[k % 4][:, 0:T], g_attn[:, k:k + 1], None, ALU.mult).then_inc(ut_dve, 1)
            dve.wait_ge(ba_done, 1)
            dve.tensor_copy(baT, banks[4][0:16, 0:T]).then_inc(ba_copied, 1)
            dve.wait_ge(ba_turned, 1)
            dve.wait_ge(zeroed, 3)
            dve.tensor_copy(ba_tok[0:META, 0, :], banks[5][0:META, 0:16])
            step(dve.tensor_copy(ba_tok[:, 1:3, :], banks[5][:, 16:48].rearrange("p (c n) -> p c n", c=2)))
            dtb3 = dt_b[:, :].unsqueeze(1).to_broadcast([P, 3, NH])
            tt(tb[:, :, :], ba_tok[:, :, NH:], dtb3, ALU.add).then_inc(gate_dve, 1)
            dve.wait_ge(gate_dve, 1)
            stt(out=ta[:, :, :], in0=tb[:, :, :], scalar=-1.0, in1=tb[:, :, :], op0=ALU.mult, op1=ALU.max)
            ts(gdec[:, :, :], tb[:, :, :], 0.0, None, ALU.max).then_inc(gate_dve, 1)
            dve.wait_ge(gate_act, 4)
            tt(gdec[:, :, :], gdec[:, :, :], ta[:, :, :], ALU.add).then_inc(gate_dve, 1)
            dve.wait_ge(gate_dve, 3)
            stt(out=gdec[:, :, :], in0=gdec[:, :, :], scalar=-1.0, in1=ea.unsqueeze(1).to_broadcast([P, 3, NH]),
                op0=ALU.mult, op1=ALU.mult).then_inc(gate_dve, 1)
            ts(beta[:, :, :], beta[:, :, :], 1.0, None, ALU.add).then_inc(gate_dve, 1)
            dve.wait_ge(gate_dve, 5)
            dve.reciprocal(beta[:, :, :], beta[:, :, :]).then_inc(gate_dve, 1)

            for n in range(QKV):
                ch = QKV_ORDER[n]
                acc = conv_acc[:, T * (n % 2):T * (n % 2 + 1)]
                dve.wait_ge((tile_read0, tile_read1)[n % 2], n // 2 + 1)
                if n >= 2:
                    dve.wait_ge(silu_done, n - 1)
                step(ts(acc, raw[:, ch, 0:T], short_w[:, 0, ch:ch + 1], None, ALU.mult))
                for j in range(1, SHORT):
                    ins = stt(out=acc, in0=raw[:, ch, j:j + T], scalar=short_w[:, j, ch:ch + 1], in1=acc,
                              op0=ALU.mult, op1=ALU.add)
                    if j < SHORT - 1:
                        step(ins)
                    else:
                        ins.then_inc(short_done, 1)

            def delta():
                dve.wait_ge(gexp_ready, 9)
                for g in GROUPS:
                    c, hh = g
                    t0, m = CHUNKS[c]
                    hs4 = slice(4 * hh, 4 * hh + 4)
                    e_up, e_rem = egs[0:m, c, 4 * hh:4 * hh + 4], egs[0:m, c, 8 + 4 * hh:12 + 4 * hh]
                    e_tot = egs[:, c, 16 + 4 * hh:20 + 4 * hh]
                    dve.wait_ge(delta_pe, PE_AT[(g, "turn")])
                    tt(ug[0:m, :, 0:m], m4(upper[0:m, 0:m]), b4(gdec[0:m, c, hs4], m), ALU.mult)
                    dve.wait_ge(delta_act, ACT_AT[(g, "turn")])
                    last = dve.tensor_reduce(kk[0:m], scratch[0:m], AX, ALU.add)
                    if c:
                        last = dve.tensor_reduce(qq[0:m], x_inv[0:m], AX, ALU.add)
                    last.then_inc(delta_dve, 1)
                    yield
                    dve.wait_ge(delta_act, ACT_AT[(g, "decay")])
                    own.then(tt(decay[0:m, :, 0:m], decay[0:m, :, 0:m], bk[5][0:m, :, 0:m], ALU.mult))
                    own.then(tt(coef_b[0:m], beta[0:m, c, hs4], rk[0:m], ALU.mult))
                    if c:
                        tt(coef_a[0:m], e_up, rk[0:m], ALU.mult)
                        own.then(tt(att[0:m, :, 0:m], att[0:m, :, 0:m], m4(upper[0:m, 0:m]), ALU.mult))
                    own.settle()
                    step(tt(coef_s[0:m], coef_b[0:m], rk[0:m], ALU.mult))
                    if c:
                        tt(att[0:m, :, 0:m], att[0:m, :, 0:m], bk[2][0:m, :, 0:m], ALU.mult)
                    tt(decay[0:m, :, 0:m], decay[0:m, :, 0:m], b4(coef_s[0:m], m), ALU.mult).then_inc(delta_dve, 1)
                    yield
                    dve.wait_ge(delta_pe, PE_AT[(g, "lvl0")])
                    tt(y_inv[0:m, :, 0:m], m4(ident[0:m, 0:m]), bk[3][0:m, :, 0:m], ALU.subtract)
                    tt(x_inv[0:m, :, 0:m], m4(ident[0:m, 0:m]), lmask[0][0:m, :, 0:m], ALU.subtract)
                    if c:
                        step(tt(scratch[0:m], bk[5][0:m], b4(coef_a[0:m]), ALU.mult))
                        own.then(tt(r_tok[0:m], r_tok[0:m], scratch[0:m], ALU.subtract))
                        tt(o_tok[0:m], bk[2][0:m], b4(e_up), ALU.mult)
                        own.settle()
                    if c < 2:
                        tt(k_tok[0:m], k_tok[0:m], b4(e_rem), ALU.mult)
                    tt(r_tok[0:m], r_tok[0:m], b4(coef_b[0:m]), ALU.mult).then_inc(delta_dve, 1)
                    yield
                    for v in range(1, n_levels(c)):
                        yield
                        dve.wait_ge(delta_pe, PE_AT[(g, f"b{v}")])
                        if v < n_levels(c) - 1:
                            tt(x_inv[0:m, :, 0:m], x_inv[0:m, :, 0:m], bk[6][0:m, :, 0:m], ALU.subtract)
                        tt(y_inv[0:m, :, 0:m], y_inv[0:m, :, 0:m], bk[4][0:m, :, 0:m], ALU.subtract
                           ).then_inc(delta_dve, 1)
                        yield
                    yield
                    dve.wait_ge(delta_pe, PE_AT[(g, "apply")])
                    if c:
                        step(tt(o_tok, o_tok, bk[4], ALU.add))
                        step(tt(scratch, o_tok, o_tok, ALU.mult))
                        step(dve.tensor_reduce(oo, scratch, AX, ALU.add))
                        ins = stt(out=oo, in0=oo, scalar=1.0 / HD ** 2, in1=rq2, op0=ALU.mult, op1=ALU.mult)
                        if c == 2:
                            ins.then_inc(delta_dve, 1)
                        else:
                            step(tt(state[:, hs4], state[:, hs4], b4(e_tot), ALU.mult))
                            tt(state[:, hs4], state[:, hs4], bk[6], ALU.add).then_inc(delta_dve, 1)
                        dve.wait_ge(delta_act, ACT_AT[(g, "norm")])
                        step(stt(out=coef_o, in0=ro, scalar=HD ** -0.5, in1=rq, op0=ALU.mult, op1=ALU.mult))
                        tt(o_tok, o_tok, b4(coef_o), ALU.mult).then_inc(delta_dve, 1)
                        yield
                        dve.wait_ge(delta_pe, PE_AT[(g, "back")])
                        z4 = mixT[:, 8 + 4 * hh:12 + 4 * hh, t0 - META:t0 - META + P]
                        stt(out=z4, in0=bk[3], scalar=g_delta, in1=z4, op0=ALU.mult, op1=ALU.mult).then_inc(delta_dve, 1)
                        yield
                    else:
                        dve.tensor_copy(state[:, hs4], bk[6]).then_inc(delta_dve, 1)
                        yield

            def conv():
                for j0 in range(0, 8, 2):
                    for tap in range(TAPS):
                        for j in (j0, j0 + 1):
                            yield j
                            acc = mixT[:, j, :]
                            if tap:
                                dve.wait_ge(conv_tap, TAPS * j0 + 2 * (tap - 1) + j - j0 + 1)
                            stt(out=acc, in0=glu[:, j, tap:tap + SEQ], scalar=dw_w[:, tap, j:j + 1],
                                in1=acc if tap else cols[:, 33 + j:34 + j].to_broadcast([P, SEQ]),
                                op0=ALU.mult, op1=ALU.add).then_inc(conv_tap, 1)
                yield 8

            n_gated = 0
            taps = conv()
            ready = next(taps)

            def some_taps(count):
                nonlocal ready
                while count > 0 and ready < n_gated:
                    ready = next(taps)
                    count -= 1

            steps = delta()
            for i, (kind, j, _, _) in enumerate(TAIL):
                for _ in range(4):
                    next(steps, None)
                    some_taps(TAPS_BETWEEN)
                n = QKV + i
                read = (tile_read0, tile_read1)[n % 2]
                if kind == "b":
                    continue
                m = j if kind == "z" else 8 + j
                width = SEQ if kind == "z" else T
                e = conv_acc[:, T * (m % 2):T * (m % 2) + width]
                if kind == "z":
                    dve.wait_ge(gate_exp, j + 1)
                else:
                    dve.wait_ge((tile_read0, tile_read1)[(n - 1) % 2], (n - 1) // 2 + 1)
                    dve.wait_ge(tile_done, n + 1)
                step(ts(e, e, 1.0, None, ALU.add))
                step(dve.reciprocal(e, e))
                if kind == "z":
                    step(tt(mixT[:, 8 + j, :], banks[n % 2][:, 0:SEQ], e, ALU.mult))
                else:
                    step(tt(glu[:, j, HISTORY:], banks[n % 2][:, 0:T], e, ALU.mult))
                dve.sem_inc(read, 1)
                dve.sem_inc(gated, 1)
                if kind == "a":
                    n_gated = j // 2 * 2 + 2 if j % 2 else n_gated
            for _ in steps:
                some_taps(TAPS_BETWEEN)
            some_taps(TAPS * 8)

            for i in range(4):
                pr = mixT[:, 2 * i:2 * i + 2, :]
                dve.wait_ge(ln_pe, i + 1)
                stt(out=pr, in0=banks[i][:, :].rearrange("p (c n) -> p c n", c=2), scalar=-1.0 / P, in1=pr,
                    op0=ALU.mult, op1=ALU.add).then_inc(ln_dve, 1)
            for i in range(4):
                pr = mixT[:, 2 * i:2 * i + 2, :]
                dve.wait_ge(ln_act, 5 + i)
                step(tt(pr, pr, ln_sq[i], ALU.mult))
                for j in (2 * i, 2 * i + 1):
                    last = ts(mixT[:, j, :], mixT[:, j, :], cols[:, 41 + j:42 + j], cols[:, 49 + j:50 + j], ALU.mult, ALU.add)
                last.then_inc(ln_dve, 1)

            dve.wait_ge(h_loaded, 16)
            for t in range(TT):
                dve.wait_ge(out_done, t + 1)
                for q in range(4):
                    v = h_res[:, t, BANK * q:BANK * (q + 1)]
                    last = tt(v, v, banks[4 * t + q][:, :], ALU.add)
                last.then_inc(h_ready, 1)
            for t in range(TT):
                dve.wait_ge(h_rstd, t + 1)
                ts(un[:, t, :], h_res[:, t, :], rsh[:, t:t + 1], None, ALU.mult).then_inc(un_ready, 1)
            for i in range(8):
                dve.wait_ge(un_turned, i + 1)
                t, g = i // 4, i % 4
                tt(uTf[:, 4 * g:4 * g + 4, P * t:P * (t + 1)], bk[i % 4], b4(g_ffn[:, 4 * g:4 * g + 4]), ALU.mult
                   ).then_inc(utf_ready, 1)

            i4 = cst[:, C_I32:C_I32 + NG]
            i32 = cst[:, C_I32:C_I32 + NE]
            dve.wait_ge(logits_turned, 1)
            dve.memset(g8[:, :, NG:], -NEG)
            step(tt(logit[:, :, :], banks[5][:, 0:72].rearrange("p (t n) -> p t n", t=TT),
                    bias36[:, :].unsqueeze(1).to_broadcast([P, TT, 36]), ALU.add))
            step(dve.tensor_copy(g8[:, :, 0:NG], logit[:, :, 0:NG]))
            for t in range(TT):
                own.then(dve.max(out=gm8[:, t, :], in_=g8[:, t, :]))
            own.settle()
            for t in range(TT):
                own.then(dve.max_index(out=idx3[:, 0, t, :], in_max=gm8[:, t, :], in_values=g8[:, t, :]))
            ts(ngm, gm8[:, :, 0], -1.0, None, ALU.mult).then_inc(route_first, 1)
            own.settle()
            step(dve.tensor_copy(gi[:, :, :], idx3[:, 0]))
            for t in range(TT):
                own.then(ts(goh[:, t, :], i4, gi[:, t, 0:1], None, ALU.is_equal))
            own.settle()
            step(ts(gneg[:, :, :], goh[:, :, :], NEG, -NEG, ALU.mult, ALU.add))
            for t in range(TT):
                e_g = es[:, t, :].rearrange("p (g n) -> p g n", g=NG)
                l_g = logit[:, t, NG:].rearrange("p (g n) -> p g n", g=NG)
                own.then(tt(e_g, l_g, goh[:, t, :].unsqueeze(2).to_broadcast([P, NG, EPG]), ALU.mult))
            own.settle()
            for t in range(TT):
                e_g = es[:, t, :].rearrange("p (g n) -> p g n", g=NG)
                own.then(tt(e_g, e_g, gneg[:, t, :].unsqueeze(2).to_broadcast([P, NG, EPG]), ALU.add))
            own.settle()
            for t in range(TT):
                own.then(dve.max(out=ev[:, t, :], in_=es[:, t, :]))
            own.settle()
            tt(dv, ev[:, :, 1], ev[:, :, 0], ALU.subtract).then_inc(route_second, 1)
            for t in range(TT):
                own.then(dve.max_index(out=idx3[:, 1, t, :], in_max=ev[:, t, :], in_values=es[:, t, :]))
            own.settle()
            step(dve.tensor_copy(ei[:, :, :], idx3[:, 1]))
            dve.wait_ge(route_act, 3)
            step(ts(w1, ex, 1.0, None, ALU.add))
            step(tt(w1, w1, pg, ALU.mult))
            step(dve.reciprocal(w1, w1))
            step(tt(w2, w1, ex, ALU.mult))
            for t in range(TT):
                own.then(ts(comb3[:, t, 0:NE], i32, ei[:, t, 0:1], w1[:, t:t + 1], ALU.is_equal, ALU.mult))
                own.then(ts(oh2[:, t, :], i32, ei[:, t, 1:2], w2[:, t:t + 1], ALU.is_equal, ALU.mult))
                own.then(ts(rank3[:, t, 0:NE], i32, ei[:, t, 0:1], None, ALU.is_equal))
                own.then(ts(oh1[:, t, :], i32, ei[:, t, 1:2], None, ALU.is_equal))
            own.settle()
            own.then(tt(comb3[:, :, 0:NE], comb3[:, :, 0:NE], oh2[:, :, :], ALU.add))
            tt(oh1[:, :, :], oh1[:, :, :], rank3[:, :, 0:NE], ALU.add).then_inc(route_dve, 1)
            dve.wait_ge(route_dve, 1)
            dve.wait_ge(route_pe, 1)
            step(stt(out=rank3[:, :, 0:NE], in0=banks[6][:, 0:2 * NE].rearrange("p (t n) -> p t n", t=TT), scalar=1.0,
                     in1=oh1[:, :, :], op0=ALU.add, op1=ALU.mult))
            step(ts(rank3[:, :, 0:NE], rank3[:, :, 0:NE], -1.0, None, ALU.add))
            step(dve.tensor_reduce(cmx, banks[6][:, 2 * NE:3 * NE], AX, ALU.max))
            for i in range(1, SEQ // CAP):
                own.then(ts(rnd[:, i - 1:i], cmx, float(i * CAP), None, ALU.is_gt))
            own.settle()
            step(dve.tensor_reduce(cmx, rnd, AX, ALU.add))
            dve.memset(hid[:, :], 0.0)
            step(ts(cmx, cmx, 1.0, None, ALU.add))
            dve.tensor_copy(rounds_i[:, :], cmx).then_inc(plan_ready, 1)

            def select(p, e):
                for t in range(TT):
                    for x_ in range(2):
                        c0 = CAP * x_
                        i64 = cst[:, C_I64:C_I64 + CAP]
                        rk_ = rank3[:, t, bass.ds(e + x_, 1)]
                        ts(sel_g[:, t, c0:c0 + CAP], i64, rk_, None, ALU.is_equal)
                        last = ts(sel_w[:, t, c0:c0 + CAP], i64, rk_, comb3[:, t, bass.ds(e + x_, 1)], ALU.is_equal, ALU.mult)
                last.then_inc(sel_ready, 1)

            def take_gathered(p):
                for g in range(4):
                    dve.wait_ge(gather_done, 4 * p + g + 1)
                    tt(uTe[:, 4 * g:4 * g + 4, :], bk[5 + g % 2], b4(g_ffn[:, 4 * g:4 * g + 4]), ALU.mult
                       ).then_inc(gather_read, 1)

            def gated_hidden(u, x_):
                dve.wait_ge(silu_gate, u + 1)
                if not isinstance(u, int) or u > 0:
                    dve.wait_ge(hid_turned, u)
                tt(hid[CAP:P, :], hs[CAP:P, :], banks[x_][CAP:P, :], ALU.mult).then_inc(hid_ready, 1)

            def take_y(u, x_):
                dve.wait_ge(down_done, u + 1)
                for v in range(2):
                    c0 = 1024 * v
                    last = dve.tensor_copy(ypair[CAP * x_:CAP * (x_ + 1), c0:c0 + BANK], banks[3][CAP * v:CAP * (v + 1), :])
                last.then_inc(y_dve, 1)

            def pair(p, e, last_pair):
                gated_hidden(2 * p, 0)
                if not last_pair:
                    dve.wait_ge(selw_turned, p + 1)
                    select(p + 1, e + 2)
                take_y(2 * p, 0)
                gated_hidden(2 * p + 1, 1)
                if not last_pair:
                    take_gathered(p + 1)
                take_y(2 * p + 1, 1)
                for i in range(8):
                    dve.wait_ge(scatter_done, 8 * p + i + 1)
                    v = h_res[:, i // 4, BANK * (i % 4):BANK * (i % 4 + 1)]
                    tt(v, v, banks[7 if i % 2 else 2][:, :], ALU.add).then_inc(scatter_read, 1)

            def one_round(r):
                if not isinstance(r, int):
                    dve.wait_ge(selw_turned, r * PAIRS)
                    nxt = ts(rank3[:, :, 0:NE], rank3[:, :, 0:NE], -float(CAP), None, ALU.add)
                    nxt.then_inc(next_ranks, 1)
                    dve.wait_ge(next_ranks, r)
                select(r * PAIRS, 0)
                take_gathered(r * PAIRS)
                if isinstance(r, int):
                    pair(0, 0, False)
                with dve.Fori(1 if isinstance(r, int) else 0, PAIRS - 1) as i:
                    pair(r * PAIRS + i, 2 * i, False)
                pair(r * PAIRS + PAIRS - 1, NE - 2, True)
            dve.wait_ge(plan_ready, 1)
            one_round(0)
            rounds = read_rounds(dve)
            with dve.If(rounds > 1):
                with dve.Fori(1, rounds) as r:
                    one_round(r)
            dve.wait_ge(scatter_read, rounds * (8 * PAIRS))
            dve.sem_inc(acc_done, 1)
            dve.wait_ge(fin_loaded, 16)
            for t in range(TT):
                dve.wait_ge(fin_act, t + 1)
                stt(out=un[:, t, :], in0=h_res[:, t, :], scalar=rsh[:, t:t + 1], in1=fin_g, op0=ALU.mult, op1=ALU.mult
                    ).then_inc(fin_dve, 1)

        @block.gpsimd
        def _(pool):
            pool.memset(glu[:, :, 0:HISTORY], 0.0).then_inc(zeroed, 1)
            pool.memset(ba_tok[:, :, :], 0.0).then_inc(zeroed, 1)
            pool.wait_ge(x_turned, KD)
            pool.memset(raw[:, :, 0:SHORT - 1], 0.0).then_inc(zeroed, 1)

            def delta():
                for g in GROUPS:
                    c, hh = g
                    m = CHUNKS[c][1]
                    for v in range(n_levels(c)):
                        if v == 0:
                            pool.wait_ge(delta_dve, DVE_AT[(g, "decay")])
                        if v == 2:
                            pool.wait_ge(delta_dve, DVE_AT[(g, "lvl0")])
                        if v == 2:
                            pool.wait_ge(delta_pe, PE_AT[(g, "lvl0")])
                        if v > 2:
                            pool.wait_ge(delta_pe, PE_AT[(g, f"a{v - 2}")])
                        pool.tensor_tensor(lmask[v % 2][0:m, :, 0:m], decay[0:m, :, 0:m], m4(mask3[0:m, v, 0:m]), ALU.mult
                                           ).then_inc(delta_pool, 1)
                        yield

            for _ in delta():
                pass


_INS = ["x", "meta", "attn_norm", "w_in", "conv_dw_w", "conv_dw_b", "conv_ln_g", "conv_ln_b", "short_conv_w",
        "a_log", "dt_bias", "delta_norm_g", "w_out", "ffn_norm", "w_group", "b_group", "w_router", "b_router",
        "w_gate", "w_up", "w_down", "final_norm"]


def kernel(**inputs):
    import numpy as _np
    import concourse.bacc as _bacc
    from concourse import mybir as _mybir
    from concourse.bass_utils import run_bass_kernel_spmd as _run

    nc = _bacc.Bacc("TRN2", target_bir_lowering=False, num_devices=1)
    arrays, args = {}, []
    named = [(n, _np.ascontiguousarray(inputs[n])) for n in _INS]
    named += list(zip(("cst_in", "masks_in"), shape_constants()))
    for name, a in named:
        arrays[f"in_{name}_dram"] = a
        args.append(nc.dram_tensor(f"in_{name}_dram", a.shape, _mybir.dt.from_np(a.dtype), kind="ExternalInput").ap())
    args.append(nc.dram_tensor("out_0_dram", (1, SEQ, D), F32, kind="ExternalOutput").ap())
    hybrid_kernel(nc, *args)
    r = _run(nc, [arrays], core_ids=[0])
    return r.results[0]["out_0_dram"]
```

```python
from contextlib import ExitStack

import concourse.bass as bass
import numpy as np
from concourse import mybir

F32 = mybir.dt.float32
I32 = mybir.dt.int32
U32 = mybir.dt.uint32
ALU = mybir.AluOpType
ACT = mybir.ActivationFunctionType
AX = mybir.AxisListType.X

P = 128
D = 2048
KD = D // P
META = 16
SEQ = 256
TT = SEQ // P
T = META + SEQ
HD = 128
NH = 8
CW = 1024
TAPS = 31
SHORT = 4
QKV = 3 * NH
NG = 4
EPG = 8
NE = NG * EPG
FE = 512
KF = FE // P
CAP = 64
EPS = 1e-6
NEG = 3e38
SLOTS = 12
SLOT = 2048
BANK = 512
PAIRS = NE // 2
HISTORY = TAPS - 1 - META

C_ID, C_UP, C_LOW, C_SUP, C_ONE, C_I64, C_I32 = 0, 128, 256, 384, 512, 640, 768
C_END = 800
LEVELS = [1, 2, 4, 8, 16, 32, 64]

CHUNKS = [(0, META), (META, P), (META + P, P)]
GROUPS = [(c, hh) for hh in range(2) for c in range(3)]


def shape_constants():
    i, j = np.arange(P)[:, None], np.arange(P)[None, :]
    cst = np.zeros((P, C_END), np.float32)
    cst[:, C_ID:C_ID + P] = i == j
    cst[:, C_UP:C_UP + P] = i <= j
    cst[:, C_LOW:C_LOW + P] = i > j
    cst[:, C_SUP:C_SUP + P] = i < j
    cst[:, C_ONE:C_ONE + P] = 1
    cst[:, C_I64:C_I64 + P] = j % CAP
    cst[:, C_I32:C_I32 + NE] = np.arange(NE)
    masks = np.zeros((P, len(LEVELS), P), np.float32)
    for n, b in enumerate(LEVELS):
        masks[:, n] = (i // (2 * b) == j // (2 * b)) & (i // b % 2 == 1) & (j // b % 2 == 0)
    return cst, masks.reshape(P, -1)


def n_levels(c):
    return 4 if c == 0 else 7


def delta_events(engine, c):
    halves = [(f"a{v}", f"b{v}") for v in range(1, n_levels(c))]
    if engine == "pe":
        return ["turn", "decay", "lvl0"] + [x for h in halves for x in h] + ["solve", "apply"] + (["back"] if c else [])
    if engine == "act":
        return ["turn", "decay"] + (["att"] if c else []) + [h[0] for h in halves] + ["solve"] + (["norm"] if c else [])
    if engine == "dve":
        return ["turn", "decay"] + (["att"] if c else []) + ["lvl0"] + [h[1] for h in halves] + ["apply"] + \
            (["scale", "back"] if c else [])
    masks = [f"mask{v}" for v in range(n_levels(c))]
    return (["keys"] if c < 2 else []) + masks[:2] + (["scores"] if c else []) + masks[2:3] + \
        (["fade"] if c == 1 else []) + masks[3:]


def delta_counts(engine):
    at, n = {}, 0
    for g in GROUPS:
        for e in delta_events(engine, g[0]):
            n += 1
            at[(g, e)] = n
    return at


PE_AT, ACT_AT, DVE_AT, POOL_AT = (delta_counts(e) for e in ("pe", "act", "dve", "pool"))

FIRST_COLUMN = {"a": 0, "b": CW, "c": 2 * CW, "z": 2 * CW + QKV * P}
BLOCKS = [("b", 0), ("a", 0)] + [("c", o + 4 * hh) for hh in range(2) for o in (8, 16, 0)] + \
    [("b", 4), ("a", 4), ("z", 0), ("z", 4)]


def tile_order():
    tiles, b = [], 0
    while b < len(BLOCKS):
        kind, first = BLOCKS[b]
        if kind == "b":
            tiles += [(k, first + j, b + i, j) for j in range(4) for i, k in enumerate("ba")]
            b += 2
        else:
            tiles += [(kind, first + j, b, j) for j in range(4)]
            b += 1
    return tiles


TILES = tile_order()
LAST_C = [max(n for n, tl in enumerate(TILES) if tl[0] == "c" and tl[1] % 8 // 4 == hh) for hh in range(2)]
C_ORDER = [tl[1] for tl in TILES if tl[0] == "c"]
TILES_THROUGH = [1 + max(n for n, tl in enumerate(TILES) if tl[2] == b) for b in range(len(BLOCKS))]
K_ORDER = list(range(8, 16)) + list(range(8))
FREED = [1 if s % 4 == 3 else len(BLOCKS) // 3 + 1 for s in range(SLOTS)]
SLOT_USES = len(BLOCKS) // 3 + 1
N_PARAMS, N_LATER = 10, 8


PAUSE_AFTER = {"turn": 1, "apply": 1}


def step_slots():
    slots = [False] * (4 * len(TILES))
    q, half = 0, -1
    for c, hh in GROUPS:
        if hh != half:
            q, half = max(q, 4 * (LAST_C[hh] + 1) + 2), hh
        for event in delta_events("pe", c):
            if q < len(slots):
                slots[q] = True
            q += 1 + PAUSE_AFTER.get(event, 0)
    return [slots[i:i + 4] for i in range(0, len(slots), 4)]


STEP_SLOTS = step_slots()
SQUARES_AFTER = 7
TAPS_BEFORE = 11
TAPS_BETWEEN = 2


def hybrid_kernel(nc, x, meta, attn_norm, w_in, conv_dw_w, conv_dw_b, conv_ln_g, conv_ln_b, short_conv_w,
                  a_log, dt_bias, delta_norm_g, w_out, ffn_norm, w_group, b_group, w_router, b_router,
                  w_gate, w_up, w_down, final_norm, cst_in, masks_in, out):
    with ExitStack() as ctx:
        def sb(name, cols, dt=F32):
            return ctx.enter_context(nc.sbuf_tensor(name, [P, cols], dt))

        def sem(name):
            return ctx.enter_context(nc.semaphore(name))

        ring = sb("ring", SLOTS * SLOT)
        region_h = sb("region_h", 4096)
        region_u = sb("region_u", KD * T)
        region_q = sb("region_q", QKV * (T + 3))
        region_y = sb("region_y", 8 * (HISTORY + T))
        region_s = sb("region_s", 1536)
        region_m = sb("region_m", 4096)
        cst = sb("cst", C_END)
        masks = sb("masks", len(LEVELS) * P)
        cols = sb("cols", 57 + 96 + 248)
        rows = sb("rows", 4 * P)
        gate_e = sb("gate_e", 2 * T)
        w_ba = sb("w_ba", KD * 16)
        w_rt = sb("w_rt", KD * 36)
        conv_acc = sb("conv_acc", 2 * T)
        lmask1 = sb("lmask1", BANK)
        bias36 = sb("bias36", 36)
        dt_b = sb("dt_b", NH)
        alog_b = sb("alog_b", NH)
        small = sb("small", 512)
        rounds_i = sb("rounds_i", 2, I32)
        idx_u = sb("idx_u", 32, U32)
        banks = [ctx.enter_context(nc.psum_tensor(f"bank{i}", [P, BANK], F32))[:, :] for i in range(8)]

        slot = [ring[:, SLOT * s:SLOT * (s + 1)] for s in range(SLOTS)]
        ident, upper, lower = cst[:, C_ID:C_ID + P], cst[:, C_UP:C_UP + P], cst[:, C_LOW:C_LOW + P]
        supper, ones = cst[:, C_SUP:C_SUP + P], cst[:, C_ONE:C_ONE + P]
        mask3 = masks[:, :].rearrange("p (l n) -> p l n", n=P)
        g_attn, g_ffn, g_delta = cols[:, 0:16], cols[:, 16:32], cols[:, 32:33]
        short_w = cols[:, 57:153].rearrange("p (j c) -> p j c", c=QKV)
        dw_w = cols[:, 153:401].rearrange("p (j c) -> p j c", c=8)

        x_in = region_q[:, 0:4096].rearrange("p (t n) -> p t n", t=TT)
        m_in = region_m[0:META, 0:D]
        junk = region_u[:, 0:D]
        uT = region_u[:, 0:KD * T].rearrange("p (k t) -> p k t", t=T)
        raw = region_q[:, :].rearrange("p (c t) -> p c t", t=T + 3)
        glu = region_y[:, :].rearrange("p (c t) -> p c t", t=HISTORY + T)
        mixT = region_m[:, :].rearrange("p (c t) -> p c t", t=SEQ)

        def temp(n, base=region_h):
            return base[:, BANK * n:BANK * (n + 1)].rearrange("p (h n) -> p h n", h=4)
        k_tok, r_tok, scratch, decay, att, ug, x_inv, y_inv = (temp(n) for n in range(8))
        state = region_s[:, 0:1024].rearrange("p (h n) -> p h n", h=8)
        lmask = [temp(2, region_s), lmask1[:, :].rearrange("p (h n) -> p h n", h=4)]
        w_tok = lmask[1]
        o_tok = ug

        h_res = region_h[:, :].rearrange("p (t n) -> p t n", t=TT)
        un = region_u[:, 0:4096].rearrange("p (t n) -> p t n", t=TT)
        uTf = [region_s[:, BANK * i:BANK * (i + 1)].rearrange("p (k t) -> p k t", k=4) for i in range(2)]
        w_slots = slot + [region_q[:, SLOT * i:SLOT * (i + 1)] for i in range(3)] + [region_y[:, 0:SLOT]]
        early = {0: region_y[:, 0:SLOT], 4: region_m[:, SLOT:2 * SLOT]}
        uTe = region_q[:, 0:2048].rearrange("p (k n) -> p k n", n=P)
        baT = region_s[0:16, 0:T]
        lgT = rows[0:36, 0:SEQ]
        ln_sq = [region_u[:, 2 * SEQ * i:2 * SEQ * (i + 1)].rearrange("p (c n) -> p c n", c=2) for i in range(4)]
        ypair = region_q[:, 4096:6144]
        hs = region_s[:, 0:512]
        hid = region_s[:, 512:1024]
        hidT = region_s[:, 1024:1536].rearrange("p (x k c) -> p x k c", x=2, c=CAP)
        sel_g = region_m[:, 0:256].rearrange("p (t n) -> p t n", t=TT)
        sel_w = region_m[:, 256:512].rearrange("p (t n) -> p t n", t=TT)
        sel_wT = region_m[:, 512:768]
        fin_g = region_m[:, 2048:4096]
        junk2 = region_y[:, 0:2048]

        ssq = small[:, 0:3]
        rstd = small[:, 3:6]
        ba_tok = small[:, 8:56].rearrange("p (c n) -> p c n", c=3)
        beta = small[:, 56:80].rearrange("p (c n) -> p c n", c=3)
        gdec = small[:, 80:104].rearrange("p (c n) -> p c n", c=3)
        ta = small[:, 104:128].rearrange("p (c n) -> p c n", c=3)
        tb = small[:, 128:152].rearrange("p (c n) -> p c n", c=3)
        ea = small[:, 152:160]
        egs = small[:, 160:232].rearrange("p (c n) -> p c n", c=3)
        kk, rk, qq, rq = (small[:, 232 + 4 * i:236 + 4 * i] for i in range(4))
        coef_s, coef_a, coef_b, coef_o = (small[:, 248 + 4 * i:252 + 4 * i] for i in range(4))
        oo, ro, rq2, lnt = (small[:, 264 + 4 * i:268 + 4 * i] for i in range(4))
        lnq = small[:, 280:284]
        logit = small[:, 0:72].rearrange("p (t n) -> p t n", t=TT)
        g8 = small[:, 72:88].rearrange("p (t n) -> p t n", t=TT)
        gm8 = small[:, 88:104].rearrange("p (t n) -> p t n", t=TT)
        gi = small[:, 104:120].rearrange("p (t n) -> p t n", t=TT)
        goh = small[:, 120:128].rearrange("p (t n) -> p t n", t=TT)
        gneg = small[:, 128:136].rearrange("p (t n) -> p t n", t=TT)
        gex = small[:, 136:144].rearrange("p (t n) -> p t n", t=TT)
        pg = small[:, 144:146]
        ngm = small[:, 146:148]
        es = small[:, 148:212].rearrange("p (t n) -> p t n", t=TT)
        ev = small[:, 212:228].rearrange("p (t n) -> p t n", t=TT)
        ei = small[:, 228:244].rearrange("p (t n) -> p t n", t=TT)
        dv = small[:, 244:246]
        ex = small[:, 246:248]
        w1 = small[:, 248:250]
        w2 = small[:, 250:252]
        oh1 = small[:, 252:316].rearrange("p (t n) -> p t n", t=TT)
        oh2 = small[:, 316:380].rearrange("p (t n) -> p t n", t=TT)
        cmx = small[:, 380:381]
        rnd = small[:, 381:384]
        ssh = small[:, 384:386]
        rsh = small[:, 386:388]
        idx3 = idx_u[:, :].rearrange("p (a t n) -> p a t n", a=2, t=TT)
        rank3 = masks[:, 0:TT * NE].rearrange("p (t n) -> p t n", t=TT)
        comb3 = masks[:, TT * NE:2 * TT * NE].rearrange("p (t n) -> p t n", t=TT)

        slot_full = [sem(f"slot_full{s}") for s in range(SLOTS)]
        slot_free = [sem(f"slot_free{s}") for s in range(SLOTS)]
        x_loaded0 = sem("x_loaded0")
        x_loaded1 = sem("x_loaded1")
        meta_loaded = sem("meta_loaded")
        params_loaded = sem("params_loaded")
        later_loaded = sem("later_loaded")
        h_loaded = sem("h_loaded")
        fin_loaded = sem("fin_loaded")
        out_stored = sem("out_stored")
        zeroed = sem("zeroed")
        rstd_ready = sem("rstd_ready")
        extra_full = [sem(f"extra_full{i}") for i in range(4)]
        early_full = {s: sem(f"early_full{s}") for s in early}
        logit_part = sem("logit_part")
        x_normed = sem("x_normed")
        x_turned = sem("x_turned")
        ut_dve = sem("ut_dve")
        ut_act = sem("ut_act")
        cols_turned = sem("cols_turned")
        cols_ready = sem("cols_ready")
        ba_done = sem("ba_done")
        ba_copied = sem("ba_copied")
        ba_turned = sem("ba_turned")
        gate_act = sem("gate_act")
        gate_dve = sem("gate_dve")
        gsum_done = sem("gsum_done")
        gexp_ready = sem("gexp_ready")
        tile_done = sem("tile_done")
        tile_read0 = sem("tile_read0")
        tile_read1 = sem("tile_read1")
        short_done = sem("short_done")
        silu_done = sem("silu_done")
        gate_exp = sem("gate_exp")
        gated = sem("gated")
        conv_tap = sem("conv_tap")
        delta_pe = sem("delta_pe")
        delta_act = sem("delta_act")
        delta_dve = sem("delta_dve")
        delta_pool = sem("delta_pool")
        ln_pe = sem("ln_pe")
        ln_dve = sem("ln_dve")
        ln_act = sem("ln_act")
        mix_done = sem("mix_done")
        out_done = sem("out_done")
        h_ready = sem("h_ready")
        h_rstd = sem("h_rstd")
        un_turned = sem("un_turned")
        utf_ready = sem("utf_ready")
        logits_done = sem("logits_done")
        logits_copied = sem("logits_copied")
        logits_turned = sem("logits_turned")
        route_dve = sem("route_dve")
        route_act = sem("route_act")
        ranks_done = sem("ranks_done")
        route_first = sem("route_first")
        route_second = sem("route_second")
        next_ranks = sem("next_ranks")
        plan_ready = sem("plan_ready")
        sel_ready = sem("sel_ready")
        gather_done = sem("gather_done")
        gather_read = sem("gather_read")
        scatter_done = sem("scatter_done")
        scatter_read = sem("scatter_read")
        selw_turned = sem("selw_turned")
        selw_ready = sem("selw_ready")
        gu_done = sem("gu_done")
        silu_gate = sem("silu_gate")
        hid_ready = sem("hid_ready")
        hid_turned = sem("hid_turned")
        hidt_ready = sem("hidt_ready")
        down_done = sem("down_done")
        y_act = sem("y_act")
        y_dve = sem("y_dve")
        order_dve = sem("order_dve")
        order_act = sem("order_act")
        fin_act = sem("fin_act")
        fin_dve = sem("fin_dve")

        class Order:

            def __init__(self, eng, s):
                self.eng, self.s, self.n, self.base = eng, s, 0, 0

            def then(self, ins):
                ins.then_inc(self.s, 1)
                self.n += 1
                return ins

            def settle(self):
                self.eng.wait_ge(self.s, self.base + self.n)

        def b4(ap, n=P):
            return ap.unsqueeze(2).to_broadcast([ap.shape[0], 4, n])

        def m4(ap):
            return ap.unsqueeze(1).to_broadcast([ap.shape[0], 4, ap.shape[1]])

        bk = [b_[:, :].rearrange("p (h n) -> p h n", h=4) for b_ in banks]
        lnh = small[:, 388:389]
        ssp = small[:, 392:396]
        ssq4 = small[:, 396:400]
        block = ctx.enter_context(nc.Block())

        w_in_v = w_in[0].rearrange("(k p) n -> p k n", p=P)
        w_out_v = w_out[0].rearrange("(k p) n -> k p n", p=P)
        gate_v = w_gate[0].rearrange("e (g k p) n -> e g p k n", p=P, k=4)
        up_v = w_up[0].rearrange("e (g k p) n -> e g p k n", p=P, k=4)
        down_v = w_down[0].rearrange("e (k p) n -> e k p n", p=P)
        x_v = x[0].rearrange("(t p) n -> p t n", p=P)
        out_v = out[0].rearrange("(t p) n -> p t n", p=P)

        def read_rounds(eng):
            eng.wait_ge(plan_ready, 1)
            return eng.value_load(rounds_i[0:1, 0:1], min_val=1, max_val=SEQ // CAP)

        @block.sync
        def _(sp):
            sp.dma_start(m_in, meta).then_inc(meta_loaded, 16)
            sp.dma_start(x_in[:, 0, :], x_v[:, 0, :]).then_inc(x_loaded0, 16)
            sp.dma_start(x_in[:, 1, :], x_v[:, 1, :]).then_inc(x_loaded1, 16)
            rows_of = ((attn_norm, 0), (ffn_norm, 16), (delta_norm_g, 32), (conv_dw_b, 33), (conv_ln_g, 41), (conv_ln_b, 49))
            loads = [(cst[:, :], cst_in)]
            loads += [(rows[r:r + a.shape[1] // P, 0:P], a[0].rearrange("(r n) -> r n", n=P)) for a, r in rows_of]
            loads.append((rows[0:96, P:2 * P], short_conv_w[0].rearrange("j (c n) -> (j c) n", n=P)))
            dw = conv_dw_w[0].rearrange("j (c n) -> (j c) n", n=P)
            loads += [(rows[0:124, P * (2 + i):P * (3 + i)], dw[124 * i:124 * (i + 1), :]) for i in range(2)]
            assert len(loads) == N_PARAMS
            for dst, src in loads:
                sp.dma_start(dst, src).then_inc(params_loaded, 16)
            for b in range(len(BLOCKS)):
                for g in range(4):
                    s = 4 * (b % 3) + g
                    if b >= 3 and g < 3:
                        sp.wait_ge(slot_free[s], b // 3)
                    elif b >= 3:
                        sp.wait_ge(tile_done, TILES_THROUGH[b - 3])
                    c0 = FIRST_COLUMN[BLOCKS[b][0]] + P * BLOCKS[b][1]
                    sp.dma_start(slot[s].rearrange("p (k n) -> p k n", k=4),
                                 w_in_v[:, 4 * g:4 * g + 4, c0:c0 + 512]).then_inc(slot_full[s], 16)
            for n, k in enumerate(K_ORDER):
                if n >= SLOTS:
                    if n == KD - 1:
                        sp.wait_ge(conv_tap, 8 * TAPS)
                    else:
                        sp.wait_ge(delta_pe, PE_AT[(GROUPS[-1], "back")])
                    sp.dma_start(w_slots[n], w_out_v[k]).then_inc(extra_full[n - SLOTS], 16)
                    continue
                if n % 4 < 3:
                    sp.wait_ge(slot_free[n], len(BLOCKS) // 3)
                else:
                    sp.wait_ge(tile_done, TILES_THROUGH[len(BLOCKS) - 3 + n // 4])
                sp.dma_start(w_slots[n], w_out_v[k]).then_inc(slot_full[n], 16)
            sp.wait_ge(delta_dve, DVE_AT[(GROUPS[-1], "back")])
            sp.dma_start(h_res, x_v).then_inc(h_loaded, 16)

            def load_expert(e, u):
                first = isinstance(u, int) and u == 0
                order = [(4 * v + g, (gate_v, up_v)[v], g) for g in range(4) for v in range(2)]
                order += [(8 + k, down_v, k) for k in range(KF)]
                for s, view, g in order:
                    if isinstance(u, int) and u == 1 and s in early:
                        sp.wait_ge(out_done, 4 * TT)
                        sp.dma_start(early[s].rearrange("p (k n) -> p k n", k=4), view[e, g]).then_inc(early_full[s], 16)
                        continue
                    if s == 7 and not first:
                        sp.wait_ge(gu_done, u)
                    elif s == 11 and not first:
                        sp.wait_ge(down_done, u)
                    else:
                        sp.wait_ge(slot_free[s], u + FREED[s] - (not first and s in early))
                    src = view[e, g]
                    dst = slot[s] if s >= 8 else slot[s].rearrange("p (k n) -> p k n", k=4)
                    sp.dma_start(dst, src).then_inc(slot_full[s], 16)
            load_expert(0, 0)
            load_expert(1, 1)
            with sp.Fori(2, NE) as e:
                load_expert(e, e)
            sp.wait_ge(gu_done, 2)
            sp.dma_start(fin_g, final_norm.partition_broadcast(P)).then_inc(fin_loaded, 16)
            rounds = read_rounds(sp)
            with sp.If(rounds > 1):
                with sp.Fori(1, rounds) as r:
                    with sp.Fori(0, NE) as e:
                        load_expert(e, r * NE + e)
            for i in range(2 * TT):
                sp.wait_ge(fin_dve, i + 1)
                v = slice(D // 2 * (i % 2), D // 2 * (i % 2 + 1))
                sp.dma_start(out_v[:, i // 2, v], un[:, i // 2, v]).then_inc(out_stored, 16)
            sp.wait_ge(out_stored, 16 * 2 * TT)

        @block.tensor
        def _(pe):
            mm, tr = nc.tensor.matmul, nc.tensor.transpose
            pe.wait_ge(params_loaded, 16 * N_PARAMS)
            for i, (n, at) in enumerate(((57, 0), (96, 57), (124, 153), (124, 277))):
                last = tr(banks[7][:, at:at + n], rows[0:n, P * i:P * (i + 1)], ident[0:n, 0:n])
            last.then_inc(cols_turned, 1)
            pe.wait_ge(x_normed, 3)
            for k in range(KD):
                if k >= 4:
                    pe.wait_ge(ut_act if k % 2 else ut_dve, (k - 4) // 2 + 1)
                b = banks[k % 4]
                tr(b[:, 0:META], m_in[:, P * k:P * (k + 1)], ident[0:META, 0:META])
                for t in range(TT):
                    last = tr(b[:, META + P * t:META + P * (t + 1)], x_in[:, t, P * k:P * (k + 1)], ident)
                last.then_inc(x_turned, 1)
            pe.wait_ge(ut_act, KD // 2)
            pe.wait_ge(ut_dve, KD // 2)

            def gate_products():
                pe.wait_ge(later_loaded, 16 * N_LATER)
                for k in range(KD):
                    last = mm(banks[4][0:16, 0:T], w_ba[:, 16 * k:16 * (k + 1)], uT[:, k, :], start=k == 0, stop=k == KD - 1)
                last.then_inc(ba_done, 1)

            def gate_turns():
                pe.wait_ge(ba_copied, 1)
                for c, (t0, m) in enumerate(CHUNKS):
                    last = tr(banks[5][0:m, 16 * c:16 * (c + 1)], baT[:, t0:t0 + m], ident[0:16, 0:16])
                last.then_inc(ba_turned, 1)

            def decay_sums():
                pe.wait_ge(gate_dve, 6)
                for c, (t0, m) in enumerate(CHUNKS):
                    o = 24 * c
                    mm(banks[6][0:m, o:o + 8], upper[0:m, 0:m], gdec[0:m, c, :], start=True, stop=True)
                    mm(banks[6][0:m, o + 8:o + 16], lower[0:m, 0:m], gdec[0:m, c, :], start=True, stop=True)
                    last = mm(banks[6][:, o + 16:o + 24], ones[0:m, :], gdec[0:m, c, :], start=True, stop=True)
                last.then_inc(gsum_done, 1)

            def project(n, b, j, width):
                if n >= 2:
                    pe.wait_ge((tile_read0, tile_read1)[n % 2], n // 2)
                for g in range(4):
                    s = 4 * (b % 3) + g
                    pe.wait_ge(slot_full[s], 16 * (b // 3 + 1))
                    for k in range(4):
                        last = mm(banks[n % 2][:, 0:width], slot[s][:, 512 * k + P * j:512 * k + P * (j + 1)],
                                  uT[:, 4 * g + k, T - width:T], start=g == k == 0, stop=g == k == 3)
                    if g == 3:
                        last.then_inc(tile_done, 1)
                    elif j == 3:
                        last.then_inc(slot_free[s], 1)
                    yield

            def delta():
                pe.wait_ge(gexp_ready, 9)
                prev = None
                for g in GROUPS:
                    c, hh = g
                    t0, m = CHUNKS[c]
                    heads = [(j, 4 * hh + j) for j in range(4)]
                    pe.wait_ge(silu_done, QKV // 2 * (hh + 1))
                    q_, k_, v_ = (lambda h, o=o: raw[:, o + h, SHORT - 1 + t0:SHORT - 1 + t0 + m] for o in (0, 8, 16))
                    if prev:
                        pe.wait_ge(delta_dve, DVE_AT[(prev, delta_events("dve", prev[0])[-1])])
                        pe.wait_ge(delta_act, ACT_AT[(prev, delta_events("act", prev[0])[-1])])
                    for j, h in heads:
                        tr(bk[2][0:m, j, :], k_(h), ident)
                        tr(bk[3][0:m, j, :], v_(h), ident)
                        if c:
                            tr(bk[4][0:m, j, :], q_(h), ident)
                        last = mm(bk[5][0:m, j, 0:m], k_(h), k_(h), start=True, stop=True)
                    last.then_inc(delta_pe, 1)
                    yield
                    pe.wait_ge(delta_dve, DVE_AT[(g, "turn")])
                    pe.wait_ge(delta_act, ACT_AT[(g, "turn")])
                    for j, h in heads:
                        last = mm(bk[6][0:m, j, 0:m], ug[0:m, j, 0:m], lower[0:m, 0:m], start=True, stop=True)
                    if c:
                        mm(banks[7][0:m, :], lower[0:m, 0:m], ug[0:m, :, 0:m], start=True, stop=True)
                        for j, h in heads:
                            last = mm(bk[2][0:m, j, 0:m], k_(h), q_(h), start=True, stop=True)
                    last.then_inc(delta_pe, 1)
                    yield
                    pe.wait_ge(delta_pool, POOL_AT[(g, "mask0")])
                    for j, h in heads:
                        last = tr(bk[3][0:m, j, 0:m], lmask[0][0:m, j, 0:m], ident[0:m, 0:m])
                    if c:
                        pe.wait_ge(delta_dve, DVE_AT[(g, "att")])
                        for j, h in heads:
                            mm(bk[5][:, j, :], k_(h), state[:, h, :], start=True, stop=True)
                            last = mm(bk[2][:, j, :], q_(h), state[:, h, :], start=True, stop=True)
                    last.then_inc(delta_pe, 1)
                    yield
                    for v in range(1, n_levels(c)):
                        pe.wait_ge(delta_pool, POOL_AT[(g, f"mask{v}")])
                        pe.wait_ge(delta_dve, DVE_AT[(g, "lvl0" if v == 1 else f"b{v - 1}")])
                        for j, h in heads:
                            last = mm(bk[3][0:m, j, 0:m], lmask[v % 2][0:m, j, 0:m], y_inv[0:m, j, 0:m],
                                      start=True, stop=True)
                        last.then_inc(delta_pe, 1)
                        yield
                        pe.wait_ge(delta_act, ACT_AT[(g, f"a{v}")])
                        for j, h in heads:
                            last = mm(bk[4][0:m, j, 0:m], x_inv[0:m, j, 0:m], scratch[0:m, j, 0:m], start=True, stop=True)
                            if v < n_levels(c) - 1:
                                last = mm(bk[6][0:m, j, 0:m], scratch[0:m, j, 0:m], x_inv[0:m, j, 0:m],
                                          start=True, stop=True)
                        last.then_inc(delta_pe, 1)
                        yield
                    pe.wait_ge(delta_dve, DVE_AT[(g, f"b{n_levels(c) - 1}")])
                    for j, h in heads:
                        last = mm(bk[7][0:m, j, :], y_inv[0:m, j, 0:m], r_tok[0:m, j, :], start=True, stop=True)
                    last.then_inc(delta_pe, 1)
                    yield
                    pe.wait_ge(delta_act, ACT_AT[(g, "solve")])
                    pe.wait_ge(delta_pool, POOL_AT[(g, "scores" if c else "keys")])
                    for j, h in heads:
                        if c < 2:
                            last = mm(bk[6][:, j, :], k_tok[0:m, j, :], w_tok[0:m, j, :], start=True, stop=True)
                        if c:
                            last = mm(bk[4][:, j, :], att[0:m, j, 0:m], w_tok[0:m, j, :], start=True, stop=True)
                    last.then_inc(delta_pe, 1)
                    yield
                    if c:
                        pe.wait_ge(delta_dve, DVE_AT[(g, "scale")])
                        for j, h in heads:
                            last = tr(bk[3][:, j, :], o_tok[:, j, :], ident)
                        last.then_inc(delta_pe, 1)
                        yield
                    prev = g

            steps = delta()
            for n, (kind, _, b, j) in enumerate(TILES):
                for quarter, _ in enumerate(project(n, b, j, SEQ if kind == "z" else T)):
                    if STEP_SLOTS[n][quarter]:
                        next(steps, None)
                if n == 4:
                    gate_products()
                if n == 5:
                    gate_turns()
                if n == 8:
                    decay_sums()
            for _ in steps:
                pass

            def project_out(t, chunks, quarters=range(4)):
                for n_k in chunks:
                    if n_k < SLOTS:
                        pe.wait_ge(slot_full[n_k], 16 * SLOT_USES)
                    else:
                        pe.wait_ge(extra_full[n_k - SLOTS], 16)
                    k = K_ORDER[n_k]
                    if k < 8 and t == 0 and k % 2 == 0:
                        pe.wait_ge(mix_done, k // 2 + 1)
                    for q in quarters:
                        last = mm(banks[4 * t + q], mixT[:, k, P * t:P * (t + 1)], w_slots[n_k][:, BANK * q:BANK * (q + 1)],
                                  start=n_k == 0, stop=n_k == KD - 1)
                        if n_k == KD - 1:
                            last.then_inc(out_done, 1)
                    if t == 1 and n_k < SLOTS:
                        last.then_inc(slot_free[n_k], 1)
                    yield

            def router(t):
                for g in range(4):
                    i = 4 * t + g
                    pe.wait_ge(h_ready, i + 1)
                    if i >= 2:
                        pe.wait_ge(utf_ready, i - 1)
                    for k in range(4):
                        last = tr(banks[g % 2][:, P * k:P * (k + 1)], h_res[:, t, P * (4 * g + k):P * (4 * g + k + 1)], ident)
                    last.then_inc(un_turned, 1)
                    yield
                    pe.wait_ge(utf_ready, i + 1)
                    if i == 0:
                        pe.wait_ge(h_ready, 3)
                    for k in range(4):
                        kk_ = 4 * g + k
                        last = mm(banks[2][0:36, P * t:P * (t + 1)], w_rt[:, 36 * kk_:36 * (kk_ + 1)], uTf[g % 2][:, k, :],
                                  start=kk_ == 0, stop=kk_ == KD - 1)
                    last.then_inc(logit_part, 1)
                    yield
                mm(banks[2][0:36, 400:401], ident[:, 0:36], ident[:, 0:1], start=True, stop=True).then_inc(logits_done, 1)
                pe.wait_ge(logits_copied, t + 1)
                tr(banks[3][:, 36 * t:36 * (t + 1)], lgT[:, P * t:P * (t + 1)], ident[0:36, 0:36]).then_inc(logits_turned, 1)
                yield

            for q, tile_read in enumerate((tile_read0, tile_read1)):
                pe.wait_ge(tile_read, len(TILES) // 2)
                for _ in project_out(0, range(4), (q,)):
                    pass
            pe.wait_ge(delta_dve, DVE_AT[(GROUPS[-1], "back")])
            for _ in project_out(0, range(4), (2, 3)):
                pass
            for i in range(4):
                pe.wait_ge(conv_tap, 2 * TAPS * (i + 1))
                mm(banks[4 + i], ones, mixT[:, 2 * i:2 * i + 2, :], start=True, stop=True).then_inc(ln_pe, 1)
            for _ in project_out(0, range(4, SQUARES_AFTER)):
                pass
            for i in range(4):
                pe.wait_ge(ln_act, i + 1)
                mm(banks[4 + i], ones, ln_sq[i], start=True, stop=True).then_inc(ln_pe, 1)
            for _ in project_out(0, range(SQUARES_AFTER, KD)):
                pass
            pe.wait_ge(ln_act, 8)
            first_router = router(0)
            for n_k, _ in enumerate(project_out(1, range(SLOTS))):
                if n_k >= 3:
                    next(first_router, None)
            for _ in first_router:
                pass
            second_router = router(1)
            for q in range(4):
                for _ in project_out(1, range(SLOTS, KD), [q]):
                    pass
                for _ in range((0, 1, 2, 2)[q]):
                    next(second_router)
            for _ in second_router:
                pass
            pe.wait_ge(route_dve, TT)
            ranks = banks[3][:, 128:128 + 3 * NE]
            mm(ranks[:, 0:NE], supper, oh1[:, 0, :], start=True, stop=True)
            mm(ranks[:, NE:2 * NE], supper, oh1[:, 1, :], start=True, stop=False)
            mm(ranks[:, NE:2 * NE], ones, oh1[:, 0, :], start=False, stop=True)
            mm(ranks[:, 2 * NE:], ones, oh1[:, 0, :], start=True, stop=False)
            mm(ranks[:, 2 * NE:], ones, oh1[:, 1, :], start=False, stop=True).then_inc(ranks_done, 1)

            def gather(p):
                pe.wait_ge(sel_ready, p + 1)
                for g in range(4):
                    if not isinstance(p, int) or p > 0 or g >= 2:
                        pe.wait_ge(gather_read, 4 * p + g - 1)
                    for k in range(4):
                        c0 = P * (4 * g + k)
                        for t in range(TT):
                            last = mm(banks[5 + g % 2][:, P * k:P * (k + 1)], un[:, t, c0:c0 + P], sel_g[:, t, :],
                                      start=t == 0, stop=t == TT - 1)
                    last.then_inc(gather_done, 1)

            def turn_weights(p):
                if not isinstance(p, int) or p > 0:
                    pe.wait_ge(scatter_read, 8 * p)
                for t in range(TT):
                    last = tr(banks[7][:, P * t:P * (t + 1)], sel_w[:, t, :], ident)
                last.then_inc(selw_turned, 1)

            def full(s, u):
                if isinstance(u, int) and u == 1 and s in early:
                    pe.wait_ge(early_full[s], 16)
                else:
                    pe.wait_ge(slot_full[s], 16 * (u + SLOT_USES + 1 - (s in early and (not isinstance(u, int) or u > 1))))

            def gate_up(u, x_):
                if not isinstance(u, int) or u >= 2:
                    pe.wait_ge(hid_ready, u - 1)
                for g in range(4):
                    full(g, u)
                    full(4 + g, u)
                    is_early = isinstance(u, int) and u == 1 and g in early
                    w_gu = [early[4 * v + g] if is_early else slot[4 * v + g] for v in range(2)]
                    for k in range(4):
                        for v in range(2):
                            last = mm(banks[x_][CAP * v:CAP * (v + 1), :], uTe[:, 4 * g + k, CAP * x_:CAP * (x_ + 1)],
                                      w_gu[v][:, 512 * k:512 * (k + 1)], start=g == k == 0, stop=g == k == 3)
                            if k == 3 and v == 1 and g == 3:
                                last.then_inc(gu_done, 1)
                            elif k == 3 and not is_early:
                                last.then_inc(slot_free[4 * v + g], 1)

            def down(u, x_):
                pe.wait_ge(hid_ready, u + 1)
                for f in range(KF):
                    last = tr(banks[2][:, P * f:P * (f + 1)], hid[:, P * f:P * (f + 1)], ident)
                last.then_inc(hid_turned, 1)
                pe.wait_ge(hidt_ready, u + 1)
                if not isinstance(u, int) or u > 0:
                    pe.wait_ge(y_act, u)
                    pe.wait_ge(y_dve, u)
                for f in range(KF):
                    full(8 + f, u)
                    for q in range(2):
                        for v in range(2):
                            c0 = 1024 * v + BANK * q
                            last = mm(banks[3 + q][CAP * v:CAP * (v + 1), :], hidT[:, x_, f, :],
                                      slot[8 + f][:, c0:c0 + BANK], start=f == 0, stop=f == KF - 1)
                    last.then_inc(slot_free[8 + f] if f < KF - 1 else down_done, 1)

            def scatter(p):
                pe.wait_ge(selw_ready, p + 1)
                pe.wait_ge(y_act, 2 * p + 2)
                pe.wait_ge(y_dve, 2 * p + 2)
                for i in range(8):
                    if i >= 2:
                        pe.wait_ge(scatter_read, 8 * p + i - 1)
                    mm(banks[7 if i % 2 else 2], sel_wT[:, P * (i // 4):P * (i // 4 + 1)],
                       ypair[:, BANK * (i % 4):BANK * (i % 4 + 1)], start=True, stop=True).then_inc(scatter_done, 1)

            def pair(p, last_pair):
                pe.wait_ge(gather_read, 4 * p + 4)
                gate_up(2 * p, 0)
                turn_weights(p)
                down(2 * p, 0)
                gate_up(2 * p + 1, 1)
                if not last_pair:
                    gather(p + 1)
                down(2 * p + 1, 1)
                scatter(p)

            def one_round(r):
                gather(r * PAIRS)
                first = isinstance(r, int)
                if first:
                    pe.wait_ge(plan_ready, 1)
                    pair(0, False)
                with pe.Fori(1 if first else 0, PAIRS - 1) as i:
                    pair(r * PAIRS + i, False)
                pair(r * PAIRS + PAIRS - 1, True)
            one_round(0)
            rounds = read_rounds(pe)
            with pe.If(rounds > 1):
                with pe.Fori(1, rounds) as r:
                    one_round(r)

        @block.scalar
        def _(act):
            act_fn = nc.scalar.activation
            own = Order(act, order_act)

            def ln_exp_table():
                act.preload_act_table_set("natural_log_exp_and_others")
            ln_exp_table()

            def rsqrt(out_, in_, scale, last_sem=None):
                own.then(act_fn(lnt_of(out_), in_, ACT.Ln, bias=EPS, scale=scale))
                own.settle()
                return act_fn(out_, lnt_of(out_), ACT.Exp, scale=-0.5)

            def lnt_of(out_):
                n = out_.shape[-1]
                return lnt[0:out_.shape[0], 0:n]

            w_rt3 = w_rt[:, :].rearrange("p (k n) -> p k n", k=KD)
            c_ba = FIRST_COLUMN["z"] + NH * P
            loads = [(w_ba[:, :].rearrange("p (k n) -> p k n", k=KD),
                      w_in[0, :, c_ba:c_ba + 2 * NH].rearrange("(k p) n -> p k n", p=P)),
                     (dt_b[:, :], dt_bias[0, :].partition_broadcast(P)),
                     (alog_b[:, :], a_log[0, :].partition_broadcast(P)),
                     (masks[:, :], masks_in),
                     (w_rt3[:, :, 0:NG], w_group[0].rearrange("(k p) n -> p k n", p=P)),
                     (w_rt3[:, :, NG:], w_router[0].rearrange("(k p) n -> p k n", p=P)),
                     (bias36[:, 0:NG], b_group[0, :].partition_broadcast(P)),
                     (bias36[:, NG:], b_router[0, :].partition_broadcast(P))]

            parts = ((m_in, meta_loaded, META), (x_in[:, 0, :], x_loaded0, P), (x_in[:, 1, :], x_loaded1, P))
            for i, (v, loaded, m) in enumerate(parts):
                act.wait_ge(loaded, 16)
                own.then(act_fn(junk[0:m], v, ACT.Square, accum_out=ssq[0:m, i:i + 1]))
                own.settle()
                rsqrt(rstd[0:m, i:i + 1], ssq[0:m, i:i + 1], 1.0 / D).then_inc(rstd_ready, 1)
            for dst, src in loads:
                act.dma_start(dst, src).then_inc(later_loaded, 16)
            act.wait_ge(cols_ready, 1)
            for k in range(1, KD, 2):
                act.wait_ge(x_turned, k + 1)
                act_fn(uT[:, k, :], banks[k % 4][:, 0:T], ACT.Copy, scale=g_attn[:, k:k + 1]).then_inc(ut_act, 1)

            def take_raw(n, i):
                act.wait_ge(tile_done, n + 1)
                if i == 0:
                    act.wait_ge(zeroed, 3)
                act_fn(raw[:, C_ORDER[i], SHORT - 1:], banks[n % 2][:, 0:T], ACT.Copy).then_inc(
                    (tile_read0, tile_read1)[n % 2], 1)

            def silu_raw(i):
                act.wait_ge(short_done, i + 1)
                act_fn(raw[:, C_ORDER[i], SHORT - 1:], conv_acc[:, T * (i % 2):T * (i % 2 + 1)], ACT.Silu
                       ).then_inc(silu_done, 1)

            def gate_logits():
                act.wait_ge(gate_dve, 2)
                act_fn(tb[:, :, :], ta[:, :, :], ACT.Exp, scale=-1.0).then_inc(gate_act, 1)
                act_fn(beta[:, :, :], ba_tok[:, :, 0:NH], ACT.Exp, scale=-1.0).then_inc(gate_act, 1)
                act.wait_ge(later_loaded, 16 * N_LATER)
                act_fn(ea, alog_b[:, :], ACT.Exp).then_inc(gate_act, 1)
                act.wait_ge(gate_act, 1)
                act_fn(ta[:, :, :], tb[:, :, :], ACT.Ln, bias=1.0).then_inc(gate_act, 1)

            def decays():
                act.wait_ge(gsum_done, 1)
                for c, (_, m) in enumerate(CHUNKS):
                    for at, n_ in ((0, m), (8, m), (16, P)):
                        act_fn(egs[0:n_, c, at:at + 8], banks[6][0:n_, 24 * c + at:24 * c + at + 8], ACT.Exp
                               ).then_inc(gexp_ready, 1)

            def delta():
                for g in GROUPS:
                    c, hh = g
                    t0, m = CHUNKS[c]
                    act.wait_ge(delta_pe, PE_AT[(g, "turn")])
                    act_fn(k_tok[0:m], bk[2][0:m], ACT.Copy)
                    act_fn(r_tok[0:m], bk[3][0:m], ACT.Copy)
                    last = act_fn(scratch[0:m], bk[2][0:m], ACT.Square)
                    if c:
                        last = act_fn(x_inv[0:m], bk[4][0:m], ACT.Square)
                    last.then_inc(delta_act, 1)
                    yield
                    act.wait_ge(delta_dve, DVE_AT[(g, "turn")])
                    own.then(act_fn(lnt[0:m], kk[0:m], ACT.Ln, bias=EPS))
                    if c:
                        own.then(act_fn(lnq[0:m], qq[0:m], ACT.Ln, bias=EPS))
                    own.settle()
                    own.then(act_fn(rk[0:m], lnt[0:m], ACT.Exp, scale=-0.5))
                    if c:
                        own.then(act_fn(rq[0:m], lnq[0:m], ACT.Exp, scale=-0.5))
                        own.then(act_fn(rq2[0:m], lnq[0:m], ACT.Exp, scale=-1.0))
                    act.wait_ge(delta_pe, PE_AT[(g, "decay")])
                    act_fn(decay[0:m, :, 0:m], bk[6][0:m, :, 0:m], ACT.Exp).then_inc(delta_act, 1)
                    if c:
                        act_fn(att[0:m, :, 0:m], bk[7][0:m, :, 0:m], ACT.Exp).then_inc(delta_act, 1)
                    yield
                    yield
                    for v in range(1, n_levels(c)):
                        act.wait_ge(delta_pe, PE_AT[(g, f"a{v}")])
                        act_fn(scratch[0:m, :, 0:m], bk[3][0:m, :, 0:m], ACT.Copy).then_inc(delta_act, 1)
                        yield
                        yield
                    act.wait_ge(delta_pe, PE_AT[(g, "solve")])
                    act_fn(w_tok[0:m], bk[7][0:m], ACT.Copy).then_inc(delta_act, 1)
                    yield
                    if c:
                        act.wait_ge(delta_dve, DVE_AT[(g, "apply")])
                        own.then(act_fn(lnt[0:m], oo[0:m], ACT.Ln, bias=EPS))
                        own.settle()
                        act_fn(ro[0:m], lnt[0:m], ACT.Exp, scale=-0.5).then_inc(delta_act, 1)
                    yield
                    if c:
                        yield

            def gate(n, kind, m):
                act.wait_ge(tile_done, n + 1)
                if m >= 2:
                    act.wait_ge(gated, m - 1)
                width = SEQ if kind == "z" else T
                return act_fn(gate_e[:, T * (m % 2):T * (m % 2) + width], banks[n % 2][:, 0:width], ACT.Exp, scale=-1.0)

            steps = delta()
            i_c = m_gate = 0
            for n, (kind, j, _, _) in enumerate(TILES):
                for _ in range(sum(STEP_SLOTS[n])):
                    next(steps, None)
                if kind == "c":
                    take_raw(n, i_c)
                    if i_c % (QKV // 2) > 0:
                        silu_raw(i_c - 1)
                    if n in LAST_C:
                        silu_raw(i_c)
                    if i_c % (QKV // 2) > 0:
                        ln_exp_table()
                    i_c += 1
                elif kind == "z":
                    gate(n, kind, m_gate).then_inc(gate_exp, 1)
                    m_gate += 1
                elif kind == "b":
                    gate(n, kind, m_gate).then_inc((tile_read0, tile_read1)[n % 2], 1)
                    m_gate += 1
                if n == 6:
                    gate_logits()
                if n == 9:
                    decays()
            for _ in steps:
                pass

            for i in range(4):
                act.wait_ge(ln_dve, i + 1)
                act_fn(ln_sq[i], mixT[:, 2 * i:2 * i + 2, :], ACT.Square).then_inc(ln_act, 1)
            for i in range(4):
                act.wait_ge(ln_pe, 5 + i)
                own.then(act_fn(ln_sq[i], banks[4 + i][:, :].rearrange("p (c n) -> p c n", c=2), ACT.Ln, bias=EPS,
                                scale=1.0 / P))
                own.settle()
                act_fn(ln_sq[i], ln_sq[i], ACT.Exp, scale=-0.5).then_inc(ln_act, 1)
            for i in range(4):
                act.wait_ge(ln_dve, 5 + i)
                act_fn(mixT[:, 2 * i:2 * i + 2, :], mixT[:, 2 * i:2 * i + 2, :], ACT.Silu).then_inc(mix_done, 1)

            ln_exp_table()
            for t in range(TT):
                for q in range(4):
                    act.wait_ge(h_ready, 4 * t + q + 1)
                    v = slice(BANK * q, BANK * (q + 1))
                    own.then(act_fn(un[:, t, v], h_res[:, t, v], ACT.Square, accum_out=ssp[:, q:q + 1]))
                own.settle()
                own.then(act_fn(ssq4, ssp, ACT.Copy, accum_out=ssh[:, t:t + 1]))
                own.settle()
                own.then(act_fn(lnh, ssh[:, t:t + 1], ACT.Ln, bias=EPS, scale=1.0 / D))
                own.settle()
                act_fn(rsh[:, t:t + 1], lnh, ACT.Exp, scale=-0.5).then_inc(h_rstd, 1)
                act.wait_ge(logits_done, t + 1)
                act_fn(lgT[:, P * t:P * (t + 1)], banks[2][0:36, P * t:P * (t + 1)], ACT.Copy).then_inc(logits_copied, 1)
                act.wait_ge(route_first, t + 1)
                act_fn(gex[:, t, :], logit[:, t, 0:NG], ACT.Exp, bias=ngm[:, t:t + 1], accum_out=pg[:, t:t + 1]
                       ).then_inc(route_act, 1)
                act.wait_ge(route_second, t + 1)
                act_fn(ex[:, t:t + 1], dv[:, t:t + 1], ACT.Exp).then_inc(route_act, 1)

            def expert(p, x_):
                u = 2 * p + x_
                act.wait_ge(gu_done, u + 1)
                if not isinstance(u, int) or u > 0:
                    act.wait_ge(hid_ready, u)
                act_fn(hs[CAP:P, :], banks[x_][0:CAP, :], ACT.Silu).then_inc(silu_gate, 1)
                if x_ == 0:
                    act.wait_ge(selw_turned, p + 1)
                    act_fn(sel_wT, banks[7][:, 0:SEQ], ACT.Copy).then_inc(selw_ready, 1)
                act.wait_ge(hid_turned, u + 1)
                act_fn(hidT[:, x_], banks[2][:, :].rearrange("p (k n) -> p k n", k=KF)[:, :, CAP:P], ACT.Copy
                       ).then_inc(hidt_ready, 1)
                act.wait_ge(down_done, u + 1)
                for v in range(2):
                    c0 = 1024 * v + BANK
                    last = act_fn(ypair[CAP * x_:CAP * (x_ + 1), c0:c0 + BANK], banks[4][CAP * v:CAP * (v + 1), :], ACT.Copy)
                last.then_inc(y_act, 1)

            def pair(p):
                expert(p, 0)
                expert(p, 1)

            act.wait_ge(plan_ready, 1)
            pair(0)
            with act.Fori(1, PAIRS) as i:
                pair(i)
            rounds = read_rounds(act)
            with act.If(rounds > 1):
                with act.Fori(1, rounds) as r:
                    with act.Fori(0, PAIRS) as i:
                        pair(r * PAIRS + i)
            ln_exp_table()
            first_added = act.value_load(rounds_i[0:1, 1:2], min_val=8 * PAIRS - 7, max_val=8 * PAIRS * (SEQ // CAP) - 7)
            for t in range(TT):
                for q in range(4):
                    act.wait_ge(scatter_read, first_added + 4 * t + q)
                    v = slice(BANK * q, BANK * (q + 1))
                    own.then(act_fn(junk2[:, v], h_res[:, t, v], ACT.Square, accum_out=ssp[:, q:q + 1]))
                own.settle()
                own.then(act_fn(ssq4, ssp, ACT.Copy, accum_out=ssh[:, t:t + 1]))
                own.settle()
                own.then(act_fn(lnh, ssh[:, t:t + 1], ACT.Ln, bias=EPS, scale=1.0 / D))
                own.settle()
                act_fn(rsh[:, t:t + 1], lnh, ACT.Exp, scale=-0.5).then_inc(fin_act, 1)

        @block.vector
        def _(dve):
            tt, ts, stt = dve.tensor_tensor, dve.tensor_scalar, dve.scalar_tensor_tensor
            own = Order(dve, order_dve)

            def step(ins):
                own.then(ins)
                own.settle()

            for i, (v, m) in enumerate(((m_in, META), (x_in[:, 0, :], P), (x_in[:, 1, :], P))):
                dve.wait_ge(rstd_ready, i + 1)
                ts(v, v, rstd[0:m, i:i + 1], None, ALU.mult).then_inc(x_normed, 1)
            dve.wait_ge(cols_turned, 1)
            dve.tensor_copy(cols[:, 0:57], banks[7][:, 0:57])
            dve.tensor_copy(cols[:, 57:153], banks[7][:, 57:153])
            dve.tensor_copy(cols[:, 153:401], banks[7][:, 153:401]).then_inc(cols_ready, 1)
            dve.wait_ge(cols_ready, 1)
            for k in range(0, KD, 2):
                dve.wait_ge(x_turned, k + 1)
                ts(uT[:, k, :], banks[k % 4][:, 0:T], g_attn[:, k:k + 1], None, ALU.mult).then_inc(ut_dve, 1)

            def gates():
                dve.wait_ge(ba_turned, 1)
                dve.wait_ge(zeroed, 3)
                dve.wait_ge(later_loaded, 16 * N_LATER)
                dve.tensor_copy(ba_tok[0:META, 0, :], banks[5][0:META, 0:16])
                step(dve.tensor_copy(ba_tok[:, 1:3, :], banks[5][:, 16:48].rearrange("p (c n) -> p c n", c=2)))
                dtb3 = dt_b[:, :].unsqueeze(1).to_broadcast([P, 3, NH])
                tt(tb[:, :, :], ba_tok[:, :, NH:], dtb3, ALU.add).then_inc(gate_dve, 1)
                dve.wait_ge(gate_dve, 1)
                stt(out=ta[:, :, :], in0=tb[:, :, :], scalar=-1.0, in1=tb[:, :, :], op0=ALU.mult, op1=ALU.max)
                ts(gdec[:, :, :], tb[:, :, :], 0.0, None, ALU.max).then_inc(gate_dve, 1)
                dve.wait_ge(gate_act, 4)
                tt(gdec[:, :, :], gdec[:, :, :], ta[:, :, :], ALU.add).then_inc(gate_dve, 1)
                dve.wait_ge(gate_dve, 3)
                stt(out=gdec[:, :, :], in0=gdec[:, :, :], scalar=-1.0, in1=ea.unsqueeze(1).to_broadcast([P, 3, NH]),
                    op0=ALU.mult, op1=ALU.mult).then_inc(gate_dve, 1)
                ts(beta[:, :, :], beta[:, :, :], 1.0, None, ALU.add).then_inc(gate_dve, 1)
                dve.wait_ge(gate_dve, 5)
                dve.reciprocal(beta[:, :, :], beta[:, :, :]).then_inc(gate_dve, 1)

            def short_conv(n, i):
                ch = C_ORDER[i]
                acc = conv_acc[:, T * (i % 2):T * (i % 2 + 1)]
                dve.wait_ge((tile_read0, tile_read1)[n % 2], n // 2 + 1)
                if i >= 2:
                    dve.wait_ge(silu_done, i - 1)
                step(ts(acc, raw[:, ch, 0:T], short_w[:, 0, ch:ch + 1], None, ALU.mult))
                for j in range(1, SHORT):
                    ins = stt(out=acc, in0=raw[:, ch, j:j + T], scalar=short_w[:, j, ch:ch + 1], in1=acc,
                              op0=ALU.mult, op1=ALU.add)
                    if j < SHORT - 1:
                        step(ins)
                    else:
                        ins.then_inc(short_done, 1)

            def delta():
                dve.wait_ge(gexp_ready, 9)
                for g in GROUPS:
                    c, hh = g
                    t0, m = CHUNKS[c]
                    hs4 = slice(4 * hh, 4 * hh + 4)
                    e_up = egs[0:m, c, hs4]
                    dve.wait_ge(delta_pe, PE_AT[(g, "turn")])
                    tt(ug[0:m, :, 0:m], m4(upper[0:m, 0:m]), b4(gdec[0:m, c, hs4], m), ALU.mult)
                    dve.wait_ge(delta_act, ACT_AT[(g, "turn")])
                    last = dve.tensor_reduce(kk[0:m], scratch[0:m], AX, ALU.add)
                    if c:
                        last = dve.tensor_reduce(qq[0:m], x_inv[0:m], AX, ALU.add)
                    last.then_inc(delta_dve, 1)
                    yield
                    dve.wait_ge(delta_act, ACT_AT[(g, "decay")])
                    own.then(tt(decay[0:m, :, 0:m], decay[0:m, :, 0:m], bk[5][0:m, :, 0:m], ALU.mult))
                    own.then(tt(coef_b[0:m], beta[0:m, c, hs4], rk[0:m], ALU.mult))
                    if c:
                        tt(coef_a[0:m], e_up, rk[0:m], ALU.mult)
                    own.settle()
                    step(tt(coef_s[0:m], coef_b[0:m], rk[0:m], ALU.mult))
                    tt(decay[0:m, :, 0:m], decay[0:m, :, 0:m], b4(coef_s[0:m], m), ALU.mult).then_inc(delta_dve, 1)
                    if c:
                        dve.wait_ge(delta_act, ACT_AT[(g, "att")])
                        tt(att[0:m, :, 0:m], att[0:m, :, 0:m], bk[2][0:m, :, 0:m], ALU.mult).then_inc(delta_dve, 1)
                    yield
                    dve.wait_ge(delta_pe, PE_AT[(g, "lvl0")])
                    tt(y_inv[0:m, :, 0:m], m4(ident[0:m, 0:m]), bk[3][0:m, :, 0:m], ALU.subtract)
                    tt(x_inv[0:m, :, 0:m], m4(ident[0:m, 0:m]), lmask[0][0:m, :, 0:m], ALU.subtract)
                    if c:
                        step(tt(scratch[0:m], bk[5][0:m], b4(coef_a[0:m]), ALU.mult))
                        own.then(tt(r_tok[0:m], r_tok[0:m], scratch[0:m], ALU.subtract))
                        tt(o_tok[0:m], bk[2][0:m], b4(e_up), ALU.mult)
                        own.settle()
                    tt(r_tok[0:m], r_tok[0:m], b4(coef_b[0:m]), ALU.mult).then_inc(delta_dve, 1)
                    yield
                    for v in range(1, n_levels(c)):
                        yield
                        dve.wait_ge(delta_pe, PE_AT[(g, f"b{v}")])
                        if v < n_levels(c) - 1:
                            tt(x_inv[0:m, :, 0:m], x_inv[0:m, :, 0:m], bk[6][0:m, :, 0:m], ALU.subtract)
                        tt(y_inv[0:m, :, 0:m], y_inv[0:m, :, 0:m], bk[4][0:m, :, 0:m], ALU.subtract
                           ).then_inc(delta_dve, 1)
                        yield
                    yield
                    dve.wait_ge(delta_pe, PE_AT[(g, "apply")])
                    if c:
                        step(tt(o_tok, o_tok, bk[4], ALU.add))
                        step(tt(scratch, o_tok, o_tok, ALU.mult))
                        step(dve.tensor_reduce(oo, scratch, AX, ALU.add))
                        ins = stt(out=oo, in0=oo, scalar=1.0 / HD ** 2, in1=rq2, op0=ALU.mult, op1=ALU.mult)
                        if c == 2:
                            ins.then_inc(delta_dve, 1)
                        else:
                            dve.wait_ge(delta_pool, POOL_AT[(g, "fade")])
                            tt(state[:, hs4], state[:, hs4], bk[6], ALU.add).then_inc(delta_dve, 1)
                        dve.wait_ge(delta_act, ACT_AT[(g, "norm")])
                        step(stt(out=coef_o, in0=ro, scalar=HD ** -0.5, in1=rq, op0=ALU.mult, op1=ALU.mult))
                        tt(o_tok, o_tok, b4(coef_o), ALU.mult).then_inc(delta_dve, 1)
                        yield
                        dve.wait_ge(delta_pe, PE_AT[(g, "back")])
                        n_z = min(max(n_silu_z - 4 * hh, 0), 4)
                        z4 = mixT[:, 8 + 4 * hh:12 + 4 * hh, t0 - META:t0 - META + P]
                        if n_z:
                            last = stt(out=z4[:, 0:n_z], in0=bk[3][:, 0:n_z], scalar=g_delta, in1=z4[:, 0:n_z],
                                       op0=ALU.mult, op1=ALU.mult)
                        if n_z < 4:
                            last = ts(z4[:, n_z:], bk[3][:, n_z:], g_delta, None, ALU.mult)
                        last.then_inc(delta_dve, 1)
                        back_done.add(g)
                        yield
                    else:
                        dve.tensor_copy(state[:, hs4], bk[6]).then_inc(delta_dve, 1)
                        yield

            def conv():
                for j0 in range(0, 8, 2):
                    for tap in range(TAPS):
                        for j in (j0, j0 + 1):
                            yield j
                            acc = mixT[:, j, :]
                            if tap:
                                dve.wait_ge(conv_tap, TAPS * j0 + 2 * (tap - 1) + j - j0 + 1)
                            stt(out=acc, in0=glu[:, j, tap:tap + SEQ], scalar=dw_w[:, tap, j:j + 1],
                                in1=acc if tap else cols[:, 33 + j:34 + j].to_broadcast([P, SEQ]),
                                op0=ALU.mult, op1=ALU.add).then_inc(conv_tap, 1)
                yield 8

            n_gated = n_silu_z = 0
            back_done = set()
            dve.wait_ge(zeroed, 1)
            taps = conv()
            ready = next(taps)

            def some_taps(count):
                nonlocal ready
                while count > 0 and ready // 2 * 2 + 1 < n_gated:
                    ready = next(taps)
                    count -= 1

            def gate(n, kind, j, m):
                nonlocal n_gated, n_silu_z
                width = SEQ if kind == "z" else T
                e = gate_e[:, T * (m % 2):T * (m % 2) + width]
                if kind == "z":
                    dve.wait_ge(gate_exp, j + 1)
                else:
                    dve.wait_ge((tile_read0, tile_read1)[(n - 1) % 2], (n - 1) // 2 + 1)
                    dve.wait_ge(tile_done, n + 1)
                step(ts(e, e, 1.0, None, ALU.add))
                step(dve.reciprocal(e, e))
                if kind == "a":
                    step(tt(glu[:, j, HISTORY:], banks[n % 2][:, 0:T], e, ALU.mult))
                    n_gated = j + 1
                else:
                    step(tt(e, banks[n % 2][:, 0:SEQ], e, ALU.mult))
                    for c in (1, 2):
                        v, ec = mixT[:, 8 + j, P * (c - 1):P * c], e[:, P * (c - 1):P * c]
                        g = (c, j // 4)
                        if g in back_done:
                            dve.wait_ge(delta_dve, DVE_AT[(g, "back")])
                            own.then(tt(v, v, ec, ALU.mult))
                        else:
                            own.then(dve.tensor_copy(v, ec))
                    own.settle()
                    n_silu_z += 1
                dve.sem_inc((tile_read0, tile_read1)[n % 2], 1)
                dve.sem_inc(gated, 1)

            steps = delta()
            i_c = m_gate = 0
            for n, (kind, j, _, _) in enumerate(TILES):
                if n > LAST_C[0]:
                    for due in STEP_SLOTS[n]:
                        if due:
                            next(steps, None)
                        some_taps(TAPS_BETWEEN)
                else:
                    some_taps(TAPS_BEFORE)
                if kind == "c":
                    short_conv(n, i_c)
                    i_c += 1
                elif kind in "az":
                    gate(n, kind, j, m_gate)
                    m_gate += 1
                if n == 4:
                    dve.wait_ge(ba_done, 1)
                    dve.tensor_copy(baT, banks[4][0:16, 0:T]).then_inc(ba_copied, 1)
                if n == 5:
                    gates()
            for _ in steps:
                some_taps(TAPS_BETWEEN)
            some_taps(TAPS * 8)

            for i in range(4):
                pr = mixT[:, 2 * i:2 * i + 2, :]
                dve.wait_ge(ln_pe, i + 1)
                stt(out=pr, in0=banks[4 + i][:, :].rearrange("p (c n) -> p c n", c=2), scalar=-1.0 / P, in1=pr,
                    op0=ALU.mult, op1=ALU.add).then_inc(ln_dve, 1)
            for i in range(4):
                pr = mixT[:, 2 * i:2 * i + 2, :]
                dve.wait_ge(ln_act, 5 + i)
                step(tt(pr, pr, ln_sq[i], ALU.mult))
                for j in (2 * i, 2 * i + 1):
                    last = ts(mixT[:, j, :], mixT[:, j, :], cols[:, 41 + j:42 + j], cols[:, 49 + j:50 + j], ALU.mult, ALU.add)
                last.then_inc(ln_dve, 1)

            i4 = cst[:, C_I32:C_I32 + NG]
            i32 = cst[:, C_I32:C_I32 + NE]

            def route(t):
                dve.wait_ge(logits_turned, t + 1)
                own.then(dve.memset(g8[:, t, NG:], -NEG))
                step(stt(out=logit[:, t, :], in0=banks[3][:, 36 * t:36 * (t + 1)], scalar=rsh[:, t:t + 1], in1=bias36[:, :],
                         op0=ALU.mult, op1=ALU.add))
                step(dve.tensor_copy(g8[:, t, 0:NG], logit[:, t, 0:NG]))
                step(dve.max(out=gm8[:, t, :], in_=g8[:, t, :]))
                ts(ngm[:, t:t + 1], gm8[:, t, 0:1], -1.0, None, ALU.mult).then_inc(route_first, 1)
                step(dve.max_index(out=idx3[:, 0, t, :], in_max=gm8[:, t, :], in_values=g8[:, t, :]))
                step(dve.tensor_copy(gi[:, t, :], idx3[:, 0, t, :]))
                step(ts(goh[:, t, :], i4, gi[:, t, 0:1], None, ALU.is_equal))
                e_g = es[:, t, :].rearrange("p (g n) -> p g n", g=NG)
                l_g = logit[:, t, NG:].rearrange("p (g n) -> p g n", g=NG)
                own.then(ts(gneg[:, t, :], goh[:, t, :], NEG, -NEG, ALU.mult, ALU.add))
                step(tt(e_g, l_g, goh[:, t, :].unsqueeze(2).to_broadcast([P, NG, EPG]), ALU.mult))
                step(tt(e_g, e_g, gneg[:, t, :].unsqueeze(2).to_broadcast([P, NG, EPG]), ALU.add))
                step(dve.max(out=ev[:, t, :], in_=es[:, t, :]))
                tt(dv[:, t:t + 1], ev[:, t, 1:2], ev[:, t, 0:1], ALU.subtract).then_inc(route_second, 1)
                step(dve.max_index(out=idx3[:, 1, t, :], in_max=ev[:, t, :], in_values=es[:, t, :]))
                step(dve.tensor_copy(ei[:, t, :], idx3[:, 1, t, :]))
                own.then(ts(rank3[:, t, 0:NE], i32, ei[:, t, 0:1], None, ALU.is_equal))
                own.then(ts(oh1[:, t, :], i32, ei[:, t, 1:2], None, ALU.is_equal))
                own.settle()
                tt(oh1[:, t, :], oh1[:, t, :], rank3[:, t, 0:NE], ALU.add).then_inc(route_dve, 1)
                dve.wait_ge(route_act, 2 * t + 2)
                w1t, w2t = w1[:, t:t + 1], w2[:, t:t + 1]
                step(ts(w1t, ex[:, t:t + 1], 1.0, None, ALU.add))
                step(tt(w1t, w1t, pg[:, t:t + 1], ALU.mult))
                step(dve.reciprocal(w1t, w1t))
                step(tt(w2t, w1t, ex[:, t:t + 1], ALU.mult))
                own.then(ts(comb3[:, t, 0:NE], i32, ei[:, t, 0:1], w1t, ALU.is_equal, ALU.mult))
                own.then(ts(oh2[:, t, :], i32, ei[:, t, 1:2], w2t, ALU.is_equal, ALU.mult))
                own.settle()
                step(tt(comb3[:, t, 0:NE], comb3[:, t, 0:NE], oh2[:, t, :], ALU.add))

            dve.wait_ge(h_loaded, 16)
            for t in range(TT):
                lag = (4, 1)[t]
                for i_q in range(4 + lag):
                    if i_q < 4:
                        dve.wait_ge(out_done, 4 * t + i_q + 1)
                        v = h_res[:, t, BANK * i_q:BANK * (i_q + 1)]
                        tt(v, v, banks[4 * t + i_q][:, :], ALU.add).then_inc(h_ready, 1)
                    if i_q >= lag:
                        g = i_q - lag
                        i = 4 * t + g
                        dve.wait_ge(un_turned, i + 1)
                        if i >= 2:
                            dve.wait_ge(logit_part, i - 1)
                        tt(uTf[g % 2], bk[g % 2], b4(g_ffn[:, 4 * g:4 * g + 4]), ALU.mult).then_inc(utf_ready, 1)
                dve.wait_ge(h_rstd, t + 1)
                ts(un[:, t, :], h_res[:, t, :], rsh[:, t:t + 1], None, ALU.mult)
                route(t)
            dve.memset(hid[:, :], 0.0)
            dve.wait_ge(route_dve, TT)
            dve.wait_ge(ranks_done, 1)
            step(stt(out=rank3[:, :, 0:NE], in0=banks[3][:, 128:128 + 2 * NE].rearrange("p (t n) -> p t n", t=TT), scalar=1.0,
                     in1=oh1[:, :, :], op0=ALU.add, op1=ALU.mult))
            step(ts(rank3[:, :, 0:NE], rank3[:, :, 0:NE], -1.0, None, ALU.add))

            def plan():
                step(dve.tensor_reduce(cmx, banks[3][:, 128 + 2 * NE:128 + 3 * NE], AX, ALU.max))
                for i in range(1, SEQ // CAP):
                    own.then(ts(rnd[:, i - 1:i], cmx, float(i * CAP), None, ALU.is_gt))
                own.settle()
                step(dve.tensor_reduce(cmx, rnd, AX, ALU.add))
                step(ts(cmx, cmx, 1.0, None, ALU.add))
                own.then(dve.tensor_copy(rounds_i[:, 0:1], cmx))
                step(ts(rnd[:, 0:1], cmx, float(8 * PAIRS), -7.0, ALU.mult, ALU.add))
                dve.tensor_copy(rounds_i[:, 1:2], rnd[:, 0:1]).then_inc(plan_ready, 1)

            def select(p, e):
                for t in range(TT):
                    for x_ in range(2):
                        c0 = CAP * x_
                        i64 = cst[:, C_I64:C_I64 + CAP]
                        rk_ = rank3[:, t, bass.ds(e + x_, 1)]
                        ts(sel_g[:, t, c0:c0 + CAP], i64, rk_, None, ALU.is_equal)
                        last = ts(sel_w[:, t, c0:c0 + CAP], i64, rk_, comb3[:, t, bass.ds(e + x_, 1)], ALU.is_equal, ALU.mult)
                last.then_inc(sel_ready, 1)

            def take_gathered(p):
                for g in range(4):
                    dve.wait_ge(gather_done, 4 * p + g + 1)
                    tt(uTe[:, 4 * g:4 * g + 4, :], bk[5 + g % 2], b4(g_ffn[:, 4 * g:4 * g + 4]), ALU.mult
                       ).then_inc(gather_read, 1)

            def gated_hidden(u, x_):
                dve.wait_ge(silu_gate, u + 1)
                if not isinstance(u, int) or u > 0:
                    dve.wait_ge(hid_turned, u)
                tt(hid[CAP:P, :], hs[CAP:P, :], banks[x_][CAP:P, :], ALU.mult).then_inc(hid_ready, 1)

            def take_y(u, x_):
                dve.wait_ge(down_done, u + 1)
                for v in range(2):
                    c0 = 1024 * v
                    last = dve.tensor_copy(ypair[CAP * x_:CAP * (x_ + 1), c0:c0 + BANK], banks[3][CAP * v:CAP * (v + 1), :])
                last.then_inc(y_dve, 1)

            def pair(p, e, last_pair):
                gated_hidden(2 * p, 0)
                if not last_pair:
                    dve.wait_ge(selw_turned, p + 1)
                    select(p + 1, e + 2)
                take_y(2 * p, 0)
                gated_hidden(2 * p + 1, 1)
                if not last_pair:
                    take_gathered(p + 1)
                take_y(2 * p + 1, 1)
                for i in range(8):
                    dve.wait_ge(scatter_done, 8 * p + i + 1)
                    v = h_res[:, i // 4, BANK * (i % 4):BANK * (i % 4 + 1)]
                    tt(v, v, banks[7 if i % 2 else 2][:, :], ALU.add).then_inc(scatter_read, 1)

            def one_round(r):
                if not isinstance(r, int):
                    dve.wait_ge(selw_turned, r * PAIRS)
                    nxt = ts(rank3[:, :, 0:NE], rank3[:, :, 0:NE], -float(CAP), None, ALU.add)
                    nxt.then_inc(next_ranks, 1)
                    dve.wait_ge(next_ranks, r)
                select(r * PAIRS, 0)
                if isinstance(r, int):
                    plan()
                take_gathered(r * PAIRS)
                if isinstance(r, int):
                    pair(0, 0, False)
                with dve.Fori(1 if isinstance(r, int) else 0, PAIRS - 1) as i:
                    pair(r * PAIRS + i, 2 * i, False)
                pair(r * PAIRS + PAIRS - 1, NE - 2, True)
            one_round(0)
            rounds = read_rounds(dve)
            with dve.If(rounds > 1):
                with dve.Fori(1, rounds) as r:
                    one_round(r)
            dve.wait_ge(fin_loaded, 16)
            for t in range(TT):
                dve.wait_ge(fin_act, t + 1)
                for v in (slice(0, D // 2), slice(D // 2, D)):
                    stt(out=un[:, t, v], in0=h_res[:, t, v], scalar=rsh[:, t:t + 1], in1=fin_g[:, v], op0=ALU.mult,
                        op1=ALU.mult).then_inc(fin_dve, 1)

        @block.gpsimd
        def _(pool):
            pool.memset(glu[:, :, 0:HISTORY], 0.0).then_inc(zeroed, 1)
            pool.memset(ba_tok[:, :, :], 0.0).then_inc(zeroed, 1)
            pool.wait_ge(x_turned, KD)
            pool.memset(raw[:, :, 0:SHORT - 1], 0.0).then_inc(zeroed, 1)

            def delta():
                for g in GROUPS:
                    c, hh = g
                    m = CHUNKS[c][1]
                    hs4 = slice(4 * hh, 4 * hh + 4)
                    for event in delta_events("pool", c):
                        if event == "keys":
                            pool.wait_ge(delta_act, ACT_AT[(g, "turn")])
                            args = (k_tok[0:m], k_tok[0:m], b4(egs[0:m, c, 8 + 4 * hh:12 + 4 * hh]))
                        elif event == "scores":
                            pool.wait_ge(delta_dve, DVE_AT[(g, "att")])
                            args = (att[0:m], att[0:m], m4(upper[0:m, 0:m]))
                        elif event == "fade":
                            args = (state[:, hs4], state[:, hs4], b4(egs[:, c, 16 + 4 * hh:20 + 4 * hh]))
                        else:
                            v = int(event[4:])
                            if v == 0:
                                pool.wait_ge(delta_dve, DVE_AT[(g, "decay")])
                            elif v == 2:
                                pool.wait_ge(delta_dve, DVE_AT[(g, "lvl0")])
                                pool.wait_ge(delta_pe, PE_AT[(g, "lvl0")])
                            elif v > 2:
                                pool.wait_ge(delta_pe, PE_AT[(g, f"a{v - 2}")])
                            args = (lmask[v % 2][0:m, :, 0:m], decay[0:m, :, 0:m], m4(mask3[0:m, v, 0:m]))
                        pool.tensor_tensor(*args, ALU.mult).then_inc(delta_pool, 1)
                        yield

            pool.wait_ge(later_loaded, 16 * N_LATER)
            pool.wait_ge(gexp_ready, 9)
            for _ in delta():
                pass


_INS = ["x", "meta", "attn_norm", "w_in", "conv_dw_w", "conv_dw_b", "conv_ln_g", "conv_ln_b", "short_conv_w",
        "a_log", "dt_bias", "delta_norm_g", "w_out", "ffn_norm", "w_group", "b_group", "w_router", "b_router",
        "w_gate", "w_up", "w_down", "final_norm"]


def kernel(**inputs):
    import numpy as _np
    import concourse.bacc as _bacc
    from concourse import mybir as _mybir
    from concourse.bass_utils import run_bass_kernel_spmd as _run

    nc = _bacc.Bacc("TRN2", target_bir_lowering=False, num_devices=1)
    arrays, args = {}, []
    named = [(n, _np.ascontiguousarray(inputs[n])) for n in _INS]
    named += list(zip(("cst_in", "masks_in"), shape_constants()))
    for name, a in named:
        arrays[f"in_{name}_dram"] = a
        args.append(nc.dram_tensor(f"in_{name}_dram", a.shape, _mybir.dt.from_np(a.dtype), kind="ExternalInput").ap())
    args.append(nc.dram_tensor("out_0_dram", (1, SEQ, D), F32, kind="ExternalOutput").ap())
    hybrid_kernel(nc, *args)
    r = _run(nc, [arrays], core_ids=[0])
    return r.results[0]["out_0_dram"]
```
